# Optimizing a Trainium2 kernel written in Bass

```python
import math, functools
import jax, jax.numpy as jnp
from jax import lax
import numpy as np

D_MODEL = 1024
BATCH = 1
SEQ = 1024
DEPTH = 1
DEC_BATCH = 8
DEC_SEQ = 4
PAST_LEN = 1024
PAGE_SIZE = 128

N_BRANCH = 4
BR_WIDTH = D_MODEL // 4
CHUNK = 128
A_GROUPS = 4
A_GDIM = BR_WIDTH // A_GROUPS
SC_WIDTH = 3
CF_WIDTH = 31
SB_HEADS = 4
SB_HDIM = BR_WIDTH // SB_HEADS
SB_BIAS_INIT = -6.0
Q_BLOCK = 128
D_FF = 2816
FFN_CONV = 3
PLE_DIM = 256
EPS = 1e-6

A_COLS = 2 * BR_WIDTH
B_COLS = 3 * BR_WIDTH
C_COLS = 2 * BR_WIDTH
D_COLS = 3 * BR_WIDTH
G_COLS = N_BRANCH * D_MODEL
IN_COLS = A_COLS + B_COLS + C_COLS + D_COLS + G_COLS
SPLITS = (A_COLS, A_COLS + B_COLS, A_COLS + B_COLS + C_COLS, A_COLS + B_COLS + C_COLS + D_COLS)

kernel_name = "hybrid_gated_branch_decoder_step"

def rmsnorm(x, g):
    xf = x.astype(jnp.float32)
    y = xf * lax.rsqrt(jnp.mean(xf * xf, axis=-1, keepdims=True) + EPS)
    return (y * g.astype(jnp.float32)).astype(x.dtype)

def layernorm(x, g, b):
    xf = x.astype(jnp.float32)
    mu = jnp.mean(xf, axis=-1, keepdims=True)
    var = jnp.mean(jnp.square(xf - mu), axis=-1, keepdims=True)
    y = (xf - mu) * lax.rsqrt(var + EPS)
    return (y * g.astype(jnp.float32) + b.astype(jnp.float32)).astype(x.dtype)

def causal_dwconv(x, w, prev):
    K = w.shape[0]
    xp = jnp.concatenate([prev.astype(x.dtype), x], axis=1)
    y = lax.conv_general_dilated(xp, w[:, None, :].astype(x.dtype), window_strides=(1,), padding='VALID',
                                 dimension_numbers=('NWC', 'WIO', 'NWC'), feature_group_count=x.shape[-1])
    return y, xp[:, xp.shape[1] - (K - 1):]

def chunk_mix(v, w_sp, b_sp, T):
    Bn, L, _ = v.shape
    vc = v.reshape(Bn, L // T, T, A_GROUPS, A_GDIM)
    w = jnp.where(jnp.tril(jnp.ones((T, T), bool)), w_sp[:, :T, :T], 0.0).astype(v.dtype)
    s = jnp.einsum('gts,bcsgd->bctgd', w, vc) + b_sp[:, :T].T[:, :, None].astype(v.dtype)
    return s.reshape(Bn, L, BR_WIDTH)

def stick_breaking(q, k, v, q_pos, bias):
    z = jnp.einsum('bqhd,bkhd->bhqk', q, k).astype(jnp.float32) * (SB_HDIM ** -0.5) \
        + bias.astype(jnp.float32)[None, :, None, None]
    k_pos = jnp.arange(k.shape[1])
    mask = k_pos[None, :] < q_pos[:, None]
    log_fail = jnp.where(mask, jax.nn.log_sigmoid(-z), 0.0)
    later = lax.cumsum(log_fail, axis=3, reverse=True) - log_fail
    a = jnp.where(mask, jnp.exp(jax.nn.log_sigmoid(z) + later), 0.0)
    return jnp.einsum('bhqk,bkhd->bqhd', a.astype(v.dtype), v)

def sb_prompt(q, k, v, bias):
    Bn, S = q.shape[:2]
    def blk(i):
        qb = lax.dynamic_slice_in_dim(q, i * Q_BLOCK, Q_BLOCK, axis=1)
        return stick_breaking(qb, k, v, i * Q_BLOCK + jnp.arange(Q_BLOCK), bias)
    o = lax.map(blk, jnp.arange(S // Q_BLOCK))
    return jnp.moveaxis(o, 0, 1).reshape(Bn, S, SB_HEADS, SB_HDIM)

def sb_sample(q, k, v, bias, cache_k, cache_v, page_table):
    Bn, T = q.shape[:2]
    past_k = cache_k[page_table].reshape(Bn, -1, SB_HEADS, SB_HDIM)
    past_v = cache_v[page_table].reshape(Bn, -1, SB_HEADS, SB_HDIM)
    past_len = past_k.shape[1]
    k_all = jnp.concatenate([past_k.astype(k.dtype), k], axis=1)
    v_all = jnp.concatenate([past_v.astype(v.dtype), v], axis=1)
    return stick_breaking(q, k_all, v_all, past_len + jnp.arange(T), bias)

def _layer(x, p, prev_b, prev_c, prev_f, attend, chunk_len,
           g_mix, w_in, ln_v_g, ln_v_b, w_sp, b_sp, conv_b_w, conv_c_w, ln_c_g, ln_c_b, sb_bias,
           w_br, w_o, g_ffn, w_up, ffn_conv_w, w_down, g_ple, w_ple_gate, w_ple):
    Bn, T, _ = x.shape
    h = rmsnorm(x, g_mix)
    a_in, b_in, c_in, d_in, gate_in = jnp.split(h @ w_in, SPLITS, axis=-1)
    u, va = jnp.split(jax.nn.gelu(a_in), 2, axis=-1)
    va = layernorm(va, ln_v_g, ln_v_b)
    out_a = u * chunk_mix(va, w_sp, b_sp, chunk_len)
    bg, cg, xb = jnp.split(b_in, 3, axis=-1)
    conv_b, new_b = causal_dwconv(cg * xb, conv_b_w, prev_b)
    out_b = bg * conv_b
    ca, cgate = jnp.split(c_in, 2, axis=-1)
    conv_c, new_c = causal_dwconv(ca * jax.nn.sigmoid(cgate), conv_c_w, prev_c)
    out_c = jax.nn.silu(layernorm(conv_c, ln_c_g, ln_c_b))
    q, k, v = [t.reshape(Bn, T, SB_HEADS, SB_HDIM) for t in jnp.split(d_in, 3, axis=-1)]
    out_d = attend(q, k, v, sb_bias).reshape(Bn, T, BR_WIDTH)
    branches = jnp.stack([out_a, out_b, out_c, out_d], axis=2)
    br = jnp.einsum('btkc,kcd->btkd', branches, w_br)
    gates = jax.nn.sigmoid(gate_in).reshape(Bn, T, N_BRANCH, D_MODEL)
    x = x + jnp.sum(gates * br, axis=2) @ w_o
    up, new_f = causal_dwconv(rmsnorm(x, g_ffn) @ w_up, ffn_conv_w, prev_f)
    ga, gb = jnp.split(up, 2, axis=-1)
    x = x + (jax.nn.silu(ga) * gb) @ w_down
    x = x + jax.nn.sigmoid(rmsnorm(x, g_ple) @ w_ple_gate) * (p @ w_ple)
    return x, k, v, va, new_b, new_c, new_f

def setup_inputs(seed: int = 0) -> dict:
    key = jax.random.key(seed)
    ks = jax.random.split(key, 40)
    n_pages = PAST_LEN // PAGE_SIZE
    n_used = DEC_BATCH * n_pages
    n_phys = n_used + n_used // 4

    def nrm(k, shape, scale=1.0):
        return scale * jax.random.normal(k, shape, jnp.float32)

    def gain(k, shape):
        return 1.0 + 0.1 * jax.random.normal(k, shape, jnp.float32)

    page_table = jax.random.permutation(ks[7], n_phys)[:n_used].reshape(DEC_BATCH, n_pages).astype(jnp.int32)
    return {
        'x_prompt': nrm(ks[0], (BATCH, SEQ, D_MODEL)),
        'x_sample': nrm(ks[1], (DEC_BATCH, DEC_SEQ, D_MODEL)),
        'p_prompt': nrm(ks[2], (DEPTH, BATCH, SEQ, PLE_DIM)),
        'p_sample': nrm(ks[3], (DEPTH, DEC_BATCH, DEC_SEQ, PLE_DIM)),
        'cache_k': nrm(ks[4], (DEPTH, n_phys, PAGE_SIZE, SB_HEADS, SB_HDIM)),
        'cache_v': nrm(ks[5], (DEPTH, n_phys, PAGE_SIZE, SB_HEADS, SB_HDIM)),
        'page_table': page_table,
        'state_conv_b': nrm(ks[8], (DEPTH, DEC_BATCH, SC_WIDTH - 1, BR_WIDTH), 0.5),
        'state_conv_c': nrm(ks[9], (DEPTH, DEC_BATCH, CF_WIDTH - 1, BR_WIDTH), 0.5),
        'state_ffn_conv': nrm(ks[10], (DEPTH, DEC_BATCH, FFN_CONV - 1, 2 * D_FF)),
        'g_mix': gain(ks[11], (DEPTH, D_MODEL)),
        'w_in': nrm(ks[12], (DEPTH, D_MODEL, IN_COLS), D_MODEL ** -0.5),
        'ln_v_g': gain(ks[13], (DEPTH, BR_WIDTH)),
        'ln_v_b': nrm(ks[14], (DEPTH, BR_WIDTH), 0.02),
        'w_sp': nrm(ks[15], (DEPTH, A_GROUPS, CHUNK, CHUNK), CHUNK ** -0.5),
        'b_sp': gain(ks[16], (DEPTH, A_GROUPS, CHUNK)),
        'conv_b_w': nrm(ks[17], (DEPTH, SC_WIDTH, BR_WIDTH), SC_WIDTH ** -0.5),
        'conv_c_w': nrm(ks[18], (DEPTH, CF_WIDTH, BR_WIDTH), CF_WIDTH ** -0.5),
        'ln_c_g': gain(ks[19], (DEPTH, BR_WIDTH)),
        'ln_c_b': nrm(ks[20], (DEPTH, BR_WIDTH), 0.02),
        'sb_bias': SB_BIAS_INIT + 0.1 * jax.random.normal(ks[31], (DEPTH, SB_HEADS), jnp.float32),
        'w_br': nrm(ks[21], (DEPTH, N_BRANCH, BR_WIDTH, D_MODEL), BR_WIDTH ** -0.5),
        'w_o': nrm(ks[22], (DEPTH, D_MODEL, D_MODEL), D_MODEL ** -0.5),
        'g_ffn': gain(ks[23], (DEPTH, D_MODEL)),
        'w_up': nrm(ks[24], (DEPTH, D_MODEL, 2 * D_FF), D_MODEL ** -0.5),
        'ffn_conv_w': nrm(ks[25], (DEPTH, FFN_CONV, 2 * D_FF), FFN_CONV ** -0.5),
        'w_down': nrm(ks[26], (DEPTH, D_FF, D_MODEL), D_FF ** -0.5),
        'g_ple': gain(ks[27], (DEPTH, D_MODEL)),
        'w_ple_gate': nrm(ks[28], (DEPTH, D_MODEL, D_MODEL), D_MODEL ** -0.5),
        'w_ple': nrm(ks[29], (DEPTH, PLE_DIM, D_MODEL), PLE_DIM ** -0.5),
        'g_final': gain(ks[30], (D_MODEL,)),
    }

def reference(x_prompt, x_sample, p_prompt, p_sample, cache_k, cache_v, page_table,
              state_conv_b, state_conv_c, state_ffn_conv,
              g_mix, w_in, ln_v_g, ln_v_b, w_sp, b_sp, conv_b_w, conv_c_w, ln_c_g, ln_c_b, sb_bias,
              w_br, w_o, g_ffn, w_up, ffn_conv_w, w_down, g_ple, w_ple_gate, w_ple, g_final):
    xp, xs = x_prompt, x_sample
    Bp, Bs, Ts = x_prompt.shape[0], x_sample.shape[0], x_sample.shape[1]
    kp, vp, cbp, ccp, cfp = [], [], [], [], []
    ks_, vs_, cvs, cbs, ccs, cfs = [], [], [], [], [], []
    for i in range(DEPTH):
        prm = (g_mix[i], w_in[i], ln_v_g[i], ln_v_b[i], w_sp[i], b_sp[i], conv_b_w[i], conv_c_w[i],
               ln_c_g[i], ln_c_b[i], sb_bias[i], w_br[i], w_o[i], g_ffn[i], w_up[i], ffn_conv_w[i], w_down[i],
               g_ple[i], w_ple_gate[i], w_ple[i])
        zb = jnp.zeros((Bp, SC_WIDTH - 1, BR_WIDTH), xp.dtype)
        zc = jnp.zeros((Bp, CF_WIDTH - 1, BR_WIDTH), xp.dtype)
        zf = jnp.zeros((Bp, FFN_CONV - 1, 2 * D_FF), xp.dtype)
        xp, k_, v_, _, nb, nc, nf = _layer(xp, p_prompt[i], zb, zc, zf, sb_prompt, CHUNK, *prm)
        kp.append(k_); vp.append(v_); cbp.append(nb); ccp.append(nc); cfp.append(nf)
        attend = functools.partial(sb_sample, cache_k=cache_k[i], cache_v=cache_v[i], page_table=page_table)
        xs, k_, v_, va, nb, nc, nf = _layer(xs, p_sample[i], state_conv_b[i], state_conv_c[i],
                                            state_ffn_conv[i], attend, Ts, *prm)
        ks_.append(k_); vs_.append(v_); cvs.append(va); cbs.append(nb); ccs.append(nc); cfs.append(nf)
    y_prompt = rmsnorm(xp, g_final)
    y_sample = rmsnorm(xs, g_final)
    return (y_prompt, y_sample,
            jnp.stack(kp), jnp.stack(vp), jnp.stack(cbp), jnp.stack(ccp), jnp.stack(cfp),
            jnp.stack(ks_), jnp.stack(vs_), jnp.stack(cvs), jnp.stack(cbs), jnp.stack(ccs), jnp.stack(cfs))


_drawn_inputs = setup_inputs


def setup_inputs(seed=0):
    import zlib

    import numpy as np

    out = dict(_drawn_inputs(seed))
    spreads = {}
    factors = {'ln_v_b': 2.929, 'ln_c_b': 8.0, 'sb_bias': 8.0, 'g_ple': 4.31}
    for name, (base, spread) in spreads.items():
        noise = np.random.default_rng([zlib.crc32(name.encode()), seed]).standard_normal(out[name].shape)
        drawn = base * np.exp(spread * noise) if base else spread * noise
        out[name] = __import__('jax').numpy.asarray(drawn.astype(out[name].dtype))
    for name, factor in factors.items():
        out[name] = (out[name] * factor).astype(out[name].dtype)
    return out
```

```python
from contextlib import ExitStack

import numpy as np

import concourse.bass as bass
from concourse import mybir

F32 = mybir.dt.float32
F32R = mybir.dt.float32r
I32 = mybir.dt.int32
ALU = mybir.AluOpType
ACT = mybir.ActivationFunctionType

P = 128
D_MODEL = 1024
KT = D_MODEL // P
TP = 1024
NB, TS = 8, 4
NS = NB * TS
T = TP + NS
CH = T // 3
NCH = 3
PC = TP - 2 * CH
W = 256
HEADS, HD = 4, 64
D_FF = 2816
FT = D_FF // P
GROUPS = (6, 6, 5, 5)
N_PAGES, PAGE = 8, 128
N_PHYS = 80
EPS = 1e-6
N_MIX = 20
N_GATE = 32
QC = 512
NEG = -1.0e30
CW = 31
LB = 2 + TP + NB * (2 + TS)
LC = (CW - 1) + TP + NB * (CW - 1 + TS)


def units_of_prompt():
    out = []
    for pair in range(HEADS // 2):
        for qc in range(TP // QC):
            for kb in reversed(range((qc + 1) * QC // P)):
                for half in range(2):
                    out.append((2 * pair + half, qc, kb))
    return out


def hybrid_layer(nc, d):
    units = units_of_prompt()
    NU = len(units)
    STEPS = NU + 1 + N_PAGES
    ctx = ExitStack()
    with ctx:
        def sem(name):
            return ctx.enter_context(nc.semaphore(name))

        base = 16512

        def at(name, shape, dt, offset):
            size = int(np.prod(shape[1:])) * 4
            assert offset % 32 == 0 and base + offset + size <= 229344, (name, offset, size)
            return nc.alloc_sbuf_tensor_at(name, shape, dt, offset=base + offset)

        w_raw = at("w_raw", [P, 2, 1280], F32, 0)
        w_hi = at("w_hi", [P, 2, 1280], F32R, 10240)
        w_lo = at("w_lo", [P, 2, 1280], F32R, 20480)
        h_hi = at("h_hi", [P, KT, T], F32R, 30720)
        h_lo = at("h_lo", [P, KT, T], F32R, 64512)
        C0 = 98304
        ident = at("ident", [P, P], F32, C0)
        mean1024 = at("mean1024", [P, P], F32, C0 + 512)
        mean256 = at("mean256", [P, P], F32, C0 + 1024)
        small = at("small", [P, 256], F32, C0 + 1536)
        ffn_w = at("ffn_w", [P, 2 * FT, 3], F32, C0 + 2560)
        ffn_state = at("ffn_state", [P, 2 * FT, NB * 2], F32, C0 + 3104)
        ffn_last = at("ffn_last", [P, 2 * FT, (NB + 1) * 2], F32, C0 + 5920)
        M0 = C0 + 9088
        X = at("X", [P, KT, T], F32, M0)
        Q0 = M0 + 33792
        g_cols = {n: small[:, 8 * i:8 * i + 8] for i, n in enumerate(("mix", "ffn", "ple", "final"))}
        eps_col = small[:, 32:33]
        sb_bias = small[:, 33:37]
        ln_c = small[:, 37:41]
        one_col = small[:, 110:111]
        conv_b_w = small[:, 41:47]
        conv_c_w = small[:, 47:47 + 2 * CW]

        q = at("q", [P, 2, T], F32, M0)
        k = at("k", [P, 2, T], F32, M0 + 8448)
        v = at("v", [P, 2, T], F32, M0 + 16896)
        vT = at("vT", [P, 9, W], F32, Q0)
        zb = at("zb", [P, 4, QC], F32, Q0 + 9216)
        le = at("le", [P, 2, QC], F32, Q0 + 17408)
        spl = at("softplus", [P, 2, QC], F32, Q0 + 21504)
        av = at("attend", [P, 3, QC], F32, Q0 + 25600)
        k_pages = at("k_pages", [P, 2, NB, 2 * PAGE], F32, Q0 + 31744)
        v_pages = at("v_pages", [P, 2, NB, W], F32, Q0 + 48128)
        A0 = Q0 + 64512
        tri = at("tri", [P, P], F32, A0)
        comp = at("comp", [P, P], F32, A0 + 512)
        causal = at("causal", [P, 2, P], F32, A0 + 1024)
        own = at("own", [P, 2, P], F32, A0 + 2048)
        bcol = at("bcol", [P, P], F32, A0 + 3072)
        qbd = at("qbd", [P, 2, NB, 2, TS], F32, A0 + 3584)
        ptab = at("ptab", [1, NB * N_PAGES], I32, A0 + 4096)

        va = at("va", [P, 2, T], F32, M0)
        side = at("side", [P, 2, T], F32, M0 + 8448)
        vaT = at("vaT", [P, 9, W], F32, M0 + 16896)
        lnv = at("lnv", [P, 2, W], F32, M0 + 26112)
        wsp = at("wsp", [P, 4, P], F32, M0 + 28160)
        bsp = at("bsp", [P, 2, P], F32, M0 + 30208)
        bss = at("bss", [P, 2, NS], F32, M0 + 31232)
        wss = at("wss", [NS, 4, NS], F32, M0 + 31488)
        stat = at("stat", [P, 9, 8], F32, M0 + 32000)
        slot_hi = at("slot_hi", [P, 2, 2, T], F32R, Q0)
        slot_lo = at("slot_lo", [P, 2, 2, T], F32R, Q0 + 16896)
        gate = at("gate", [P, NCH, CH], F32, Q0 + 33792)
        u = at("u", [P, 2, T], F32, Q0 + 38016)
        bg = at("bg", [P, 2, T], F32, Q0 + 38016)
        pb = at("pb", [P, 2, LB], F32, Q0 + 46464)
        pcv = at("pc", [P, 2, LC], F32, Q0 + 55072)
        acc = at("conv_sum", [P, LC - CW + 1], F32, Q0 + 65696)
        cv = at("cv", [P, 2, T], F32, Q0 + 55072)
        csq = at("csq", [P, 2, CH], F32, Q0 + 65696)
        cstd = at("cstd", [P, CH], F32, Q0 + 65696 + 2816)
        x_again = at("x_again", [P, KT, T], F32, Q0 + 33792)
        hid_hi = at("hid_hi", [P, 6, T], F32R, Q0)
        hid_lo = at("hid_lo", [P, 6, T], F32R, Q0 + 25344)
        up = at("up", [P, 2, LB], F32, Q0 + 50688)
        cu = at("cu", [P, 2, LB - 2], F32, Q0 + 59296)
        p_in = at("p_in", [P, 2, T], F32, Q0 + 50688)
        p_lo = at("p_lo", [P, 2, T], F32R, Q0 + 50688)
        p_hi = at("p_hi", [P, 2, T], F32R, Q0 + 59136)
        NT = Q0
        sq = at("sq", [P, 2, CH], F32, NT)
        ssum = at("ssum", [P, 2, CH], F32, NT + 2816)
        rstd = at("rstd", [P, 2, CH], F32, NT + 5632)
        nt = at("nt", [P, 4, CH], F32, NT + 8448)

        ps = ctx.enter_context(nc.psum_tensor("ps", [P, 8, 512], F32))

        w_in = [sem("w_in0"), sem("w_in1")]
        w_high = sem("w_high")
        w_split = sem("w_split")
        x_in = [sem(f"x_in{c}") for c in range(NCH)]
        consts_in = sem("consts_in")
        att_in = sem("att_in")
        mixc_in = sem("mixc_in")
        x2_in = sem("x2_in")
        a_full = sem("a_full")
        a_read = sem("a_read")
        d_full = sem("d_full")
        d_read = sem("d_read")
        n_sq = sem("n_sq")
        n_add = sem("n_add")
        n_sum = sem("n_sum")
        n_std = sem("n_std")
        n_t = sem("n_t")
        n_hi = sem("n_hi")
        n_lo = sem("n_lo")
        tr_full, tr_read = sem("tr_full"), sem("tr_read")
        z_full, z_read = sem("z_full"), sem("z_read")
        lch = sem("lch")
        l_ready, sp_ready = sem("l_ready"), sem("sp_ready")
        later_full, t_ready = sem("later_full"), sem("t_ready")
        a_ready, pv_done = sem("a_ready"), sem("pv_done")
        o_read = sem("o_read")
        qbd_ready = sem("qbd_ready")
        kp_in = [sem(f"kp_in{g}") for g in range(2)]
        vp_in = [sem(f"vp_in{g}") for g in range(2)]
        dch = sem("dch")
        slot_ready = sem("slot_ready")
        out_kv = sem("out_kv")
        out_state = sem("out_state")
        out_va = sem("out_va")
        out_last = sem("out_last")
        out_y = [sem(f"out_y{n}") for n in range(4)]
        va_stat, va_std, va_done = sem("va_stat"), sem("va_std"), sem("va_done")
        mix_full, mix_read = sem("mix_full"), sem("mix_read")
        tables_masked = sem("tables_masked")
        pads_ready = sem("pads_ready")
        prod_done = sem("prod_done")
        c_conv, c_mean, c_cent, c_sq, c_var, c_std, c_norm, c_act = (sem(n) for n in (
            "c_conv", "c_mean", "c_cent", "c_sq", "c_var", "c_std", "c_norm", "c_act"))
        g_used = sem("g_used")
        m_ready = sem("m_ready")
        up_used = sem("up_used")
        ga_act, prod_ready, hid_h, hid_ready = (sem(n) for n in (
            "ga_act", "prod_ready", "hid_h", "hid_ready"))
        p_land = sem("p_land")
        p_ready = sem("p_ready")

        phases = [("w_mix", 0, N_MIX, 1024), ("w_gate", 0, N_GATE, 1280), ("w_o", 0, KT, 1024)]
        f0 = 0
        for n, g in enumerate(GROUPS):
            phases += [("w_up", 2 * f0, 2 * g, 1024), ("w_down", KT * n, KT, 128 * g)]
            f0 += g
        phases += [("w_ple", 0, KT, 1280)]
        first_tile = []
        n_tiles = 0
        for _, _, n, _ in phases:
            first_tile.append(n_tiles)
            n_tiles += n
        done_with = []
        na = nd = 0
        for name, _, n, _ in phases:
            if name in ("w_mix", "w_up"):
                done_with.append((a_full, na))
                na += n
            else:
                done_with.append((d_full, nd))
                nd += n
                na += n if name in ("w_gate", "w_ple") else 0

        def tokens(c):
            return slice(c * CH, (c + 1) * CH)

        def sample_cols(buf, pad):
            a = pad + TP
            return buf[:, a:a + NB * (pad + TS)].rearrange("p (b t) -> p b t", b=NB)[:, :, pad:]

        def sample_states(buf, pad):
            a = pad + TP
            return buf[:, a:a + NB * (pad + TS)].rearrange("p (b t) -> p b t", b=NB)[:, :, :pad]

        def last_cols(buf, pad):
            return buf[:, TP - TS:].rearrange("p (b t) -> p b t", b=NB + 1)[:, :, TS:]

        def as_samples(ap):
            return ap.rearrange("p (b t) -> p b t", b=NB)


        def normed_tiles(ph):
            return sum(n for name, _, n, _ in phases[:ph] if name in ("w_mix", "w_gate", "w_up"))

        def d_tiles(ph):
            return sum(n for name, _, n, _ in phases[:ph] if name not in ("w_mix", "w_up"))

        UP = [3 + 2 * g for g in range(len(GROUPS))]
        DOWN = [4 + 2 * g for g in range(len(GROUPS))]
        PLE = len(phases) - 1

        def offset(i):
            _, qc, kb = units[i]
            return max(0, kb * P - qc * QC)

        def width(i):
            return slice(offset(i), QC) if i < NU else slice(0, P)

        def keys(i):
            return NS if i == NU else P

        def is_first(i):
            return units[i][2] == (units[i][1] + 1) * QC // P - 1 if i < NU else i == NU

        def is_last(i):
            return units[i][2] == 0 if i < NU else i == STEPS - 1

        def on_diagonal(i):
            return units[i][2] * P >= units[i][1] * QC if i < NU else i == NU

        def chains_before(i):
            return sum(1 for j in range(min(i, STEPS)) if is_last(j))

        block = ctx.enter_context(nc.Block())

        @block.sync
        def _(sp):
            def weights(ph, p0=0, p1=None):
                name, t0, n, cols = phases[ph]
                b = first_tile[ph]
                p1 = n // 2 if p1 is None else p1

                def one(p, j):
                    src = d[name][bass.ds(p * 2 + (t0 + j), 1), :, 0:cols]
                    sp.dma_start(w_raw[:, j, 0:cols], src.rearrange("a p n -> p (a n)")
                                 ).then_inc(w_in[j], 16)

                if b == 0 and p0 == 0:
                    one(0, 0)
                    one(0, 1)
                    p0 = 1
                with sp.Fori(p0, p1) as p:
                    for j in range(2):
                        sp.wait_ge(w_split, p * 2 + (b + j - 1))
                        one(p, j)

            sp.dma_start(X[:, :, tokens(0)], d["x"][0]).then_inc(x_in[0], 16)
            for name, dst in (("small", small), ("mean1024", mean1024), ("mean256", mean256),
                              ("ident", ident), ("ffn_w", ffn_w), ("ffn_state", ffn_state)):
                sp.dma_start(dst[:], d[name]).then_inc(consts_in, 16)
            sp.dma_start(X[:, :, tokens(1)], d["x"][1]).then_inc(x_in[1], 16)
            sp.dma_start(X[:, :, tokens(2)], d["x"][2]).then_inc(x_in[2], 16)
            for name, dst in (("tri", tri), ("comp", comp), ("causal", causal), ("own", own),
                              ("bcol", bcol), ("ptab", ptab)):
                sp.dma_start(dst[:], d[name]).then_inc(att_in, 16)
            weights(0, 0, 4)
            sp.wait_ge(att_in, 16 * 6)

            def pages(g, cache, ring, landed):
                page = N_PAGES - 1 - g
                for b in range(NB):
                    phys = sp.value_load(ptab[0:1, b * N_PAGES + page:b * N_PAGES + page + 1],
                                         min_val=0, max_val=N_PHYS - 1)
                    src = d[cache][bass.ds(phys, 1)].rearrange("a p n -> p (a n)")
                    sp.dma_start(ring[:, g % 2, b, :], src).then_inc(landed[g % 2], 16)

            for g in range(N_PAGES + 3):
                if g < N_PAGES:
                    if g >= 2:
                        sp.wait_ge(z_full, NU + g)
                    pages(g, "cache_kT", k_pages, kp_in)
                if g >= 3:
                    if g >= 5:
                        sp.wait_ge(pv_done, NU + g - 3)
                    pages(g - 3, "cache_v", v_pages, vp_in)
            sp.wait_ge(slot_ready, 1)
            sp.wait_ge(out_kv, 16 * 2)
            for name, dst in (("lnv", lnv), ("wsp", wsp), ("bsp", bsp), ("bss", bss), ("wss", wss)):
                sp.dma_start(dst[:], d[name]).then_inc(mixc_in, 16)
            for t in range(2):
                sp.dma_start(sample_states(pb[:, t, :], 2), d["state_b"][t]).then_inc(mixc_in, 16)
                sp.dma_start(sample_states(pcv[:, t, :], CW - 1), d["state_c"][t]
                             ).then_inc(mixc_in, 16)
            weights(0, 4)
            weights(1)
            sp.wait_ge(m_ready, 1)
            sp.wait_ge(out_state, 16 * 4)
            for c in range(NCH):
                sp.dma_start(x_again[:, :, tokens(c)], d["x"][c]).then_inc(x2_in, 16)
            for ph in range(2, PLE):
                weights(ph)
            sp.wait_ge(up_used, 2 * FT + 2)
            sp.wait_ge(hid_ready, FT)
            sp.dma_start(p_in[:], d["p"]).then_inc(p_land, 16)
            weights(PLE)

        @block.gpsimd
        def _(pool):
            def split(ph, p0=0, p1=None):
                _, _, n, cols = phases[ph]
                b = first_tile[ph]
                p1 = n // 2 if p1 is None else p1

                def one(p, j):
                    pool.wait_ge(w_in[j], p * 16 + 16 * (b // 2 + 1))
                    raw, hi, lo = w_raw[:, j, 0:cols], w_hi[:, j, 0:cols], w_lo[:, j, 0:cols]
                    pool.tensor_tensor(hi, raw, one_col.to_broadcast([P, cols]), ALU.mult
                                       ).then_inc(w_high, 1)
                    pool.wait_ge(w_high, p * 2 + (b + j + 1))
                    pool.tensor_tensor(lo, raw, hi, ALU.subtract).then_inc(w_split, 1)

                if p0 == 0:
                    for j in range(2):
                        if ph > 0:
                            s, first = done_with[ph - 1]
                            pool.wait_ge(s, 3 * (first + phases[ph - 1][2] - 1 + j))
                        one(0, j)
                    p0 = 1
                s, first = done_with[ph]
                with pool.Fori(p0, p1) as p:
                    for j in range(2):
                        pool.wait_ge(s, p * 6 + 3 * (first + j - 1))
                        one(p, j)

            pool.wait_ge(consts_in, 16 * 6)
            split(0, 0, 4)
            pool.wait_ge(mixc_in, 16 * 9)
            pool.affine_select(out=wsp[:], in_=wsp[:], compare_op=ALU.is_ge, fill=0.0, base=0,
                               pattern=[[0, 4], [1, P]], channel_multiplier=-1
                               ).then_inc(tables_masked, 1)
            pool.affine_select(out=wss[:], in_=wss[:], compare_op=ALU.is_ge, fill=0.0, base=0,
                               pattern=[[0, 4], [1, NS]], channel_multiplier=-1
                               ).then_inc(tables_masked, 1)
            split(0, 4)
            for ph in range(1, len(phases)):
                split(ph)

        @block.tensor
        def _(pe):
            def product(j, blocks, rhs_hi, rhs_lo, out, full):
                last = 3 * len(blocks) - 1
                m = 0
                for i, b in enumerate(blocks):
                    wh = w_hi[:, j, b * P:(b + 1) * P]
                    wl = w_lo[:, j, b * P:(b + 1) * P]
                    for w_, r_ in ((wh, rhs_hi(i)), (wh, rhs_lo(i)), (wl, rhs_hi(i))):
                        mm = pe.matmul(out, w_, r_, start=(m == 0), stop=(m == last))
                        m += 1
                mm.then_inc(full, 1)

            def norm_sums(n):
                for c in range(NCH):
                    pe.wait_ge(n_add, 7 * (NCH * n + c + 1))
                    pe.matmul(ps[:, 6 + (NCH * n + c) % 2, 0:CH], mean1024[:],
                              ssum[:, (NCH * n + c) % 2, :], start=True, stop=True
                              ).then_inc(n_sum, 1)

            def a_tile(p, j, b, a, norm=None):
                for c in range(NCH):
                    if c == 0:
                        pe.wait_ge(w_split, p * 2 + (b + j + 1))
                    if norm is not None:
                        pe.wait_ge(n_lo, 24 * norm + 8 * (c + 1))
                    if norm != 0:
                        pe.wait_ge(a_read, a * 3 + (c - 2))
                    product(j, range(8), lambda i: h_hi[:, i, tokens(c)],
                            lambda i: h_lo[:, i, tokens(c)], ps[:, c, 0:CH], a_full)

            def d_tile(j, dn, blocks, rhs_hi, rhs_lo):
                for c in range(NCH):
                    if not (isinstance(dn, int) and dn == 0):
                        pe.wait_ge(d_read, dn * 3 + (c - 2))
                    product(j, blocks, lambda i: rhs_hi(i, c), lambda i: rhs_lo(i, c),
                            ps[:, 3 + c, 0:CH], d_full)

            def transposes(src, n0):
                for blk in range(9):
                    w_ = P if blk < 8 else NS
                    n = n0 + blk
                    if n >= 2:
                        pe.wait_ge(tr_read, n - 1)
                    for t in range(2):
                        mm = pe.transpose(ps[0:w_, 6 + n % 2, t * P:(t + 1) * P],
                                          src[:, t, blk * P:blk * P + w_], ident[:])
                    mm.then_inc(tr_full, 1)

            pe.wait_ge(consts_in, 16 * 6)
            norm_sums(0)
            for n in range(6):
                a_tile(n // 2, n % 2, 0, n, norm=0 if n == 0 else None)
            pe.wait_ge(a_read, 18)
            transposes(v, 0)

            pe.wait_ge(att_in, 16 * 6)
            pe.wait_ge(tr_read, 9)

            def scores(i):
                if i >= 2:
                    pe.wait_ge(z_read, i - 1)
                bank = 5 + i % 2
                if i < NU:
                    h, qc, kb = units[i]
                    r = slice(HD * (h % 2), HD * (h % 2) + HD)
                    mm = pe.matmul(ps[:, bank, width(i)], k[r, h // 2, kb * P:(kb + 1) * P],
                                   q[r, h // 2, qc * QC + offset(i):(qc + 1) * QC],
                                   start=True, stop=True)
                elif i == NU:
                    pe.wait_ge(qbd_ready, 1)
                    for hp in range(2):
                        mm = pe.matmul(ps[0:NS, bank, hp * 64:(hp + 1) * 64], k[:, hp, TP:T],
                                       qbd[:, hp].rearrange("p b h t -> p (b h t)"),
                                       start=True, stop=True)
                else:
                    g = i - NU - 1
                    pe.wait_ge(kp_in[g % 2], 16 * NB * (g // 2 + 1))
                    for hp in range(2):
                        for b in range(NB):
                            col = hp * 64 + b * 8
                            mm = pe.matmul(ps[:, bank, col:col + 8],
                                           k_pages[:, g % 2, b, hp * PAGE:(hp + 1) * PAGE],
                                           qbd[:, hp, b].rearrange("p h t -> p (h t)"),
                                           start=True, stop=True)
                mm.then_inc(z_full, 1)

            def chain_bank(i):
                return 3 + units[i][0] % 2 if i < NU else 3

            def later(i):
                pe.wait_ge(sp_ready, i + 1)
                n = keys(i)
                pe.matmul(ps[:, chain_bank(i), width(i)], tri[0:n, :], spl[0:n, i % 2, width(i)],
                          start=is_first(i), stop=is_last(i), skip_group_check=True
                          ).then_inc(later_full, 1)

            def rest(i):
                pe.wait_ge(t_ready, i + 1)
                if not is_last(i):
                    n = keys(i)
                    pe.matmul(ps[:, chain_bank(i), width(i)], comp[0:n, :],
                              spl[0:n, i % 2, width(i)], start=False, stop=False,
                              skip_group_check=True)

            def values(i):
                pe.wait_ge(a_ready, i + 1)
                if is_first(i) and chains_before(i):
                    pe.wait_ge(o_read, chains_before(i))
                if i < NU:
                    h, qc, kb = units[i]
                    r = HD * (h % 2)
                    mm = pe.matmul(ps[r:r + HD, 7, width(i)], vT[:, kb, h * HD:(h + 1) * HD],
                                   av[:, i % 3, width(i)], start=is_first(i), stop=is_last(i),
                                   skip_group_check=True)
                elif i == NU:
                    for hp in range(2):
                        mm = pe.matmul(ps[:, 7, hp * 64:(hp + 1) * 64],
                                       vT[0:NS, 8, hp * P:(hp + 1) * P],
                                       av[0:NS, i % 3, hp * 64:(hp + 1) * 64],
                                       start=(hp == 0), stop=False, skip_group_check=True)
                else:
                    g = i - NU - 1
                    pe.wait_ge(vp_in[g % 2], 16 * NB * (g // 2 + 1))
                    for hp in range(2):
                        for b in range(NB):
                            col = hp * 64 + b * 8
                            mm = pe.matmul(ps[:, 7, col:col + 8],
                                           v_pages[:, g % 2, b, hp * P:(hp + 1) * P],
                                           av[:, i % 3, col:col + 8], start=False,
                                           stop=is_last(i), skip_group_check=True)
                mm.then_inc(pv_done, 1)

            scores(0)
            scores(1)
            for i in range(STEPS + 2):
                if i + 2 < STEPS:
                    scores(i + 2)
                if 1 <= i <= STEPS:
                    rest(i - 1)
                if i < STEPS:
                    later(i)
                if i >= 2:
                    values(i - 2)

            for n in range(6, 18):
                a_tile(n // 2, n % 2, 0, n)
            pe.wait_ge(o_read, chains_before(STEPS))
            transposes(va, 9)
            pe.wait_ge(va_done, 9)
            pe.wait_ge(tables_masked, 2)
            for t in range(2):
                for half in range(2):
                    for c4 in range(4):
                        for g in range(2):
                            mm = pe.matmul(ps[64 * g:64 * g + 64, 3 + 2 * t + half,
                                              c4 * P:(c4 + 1) * P],
                                           vaT[:, 4 * half + c4, (2 * t + g) * 64:(2 * t + g + 1) * 64],
                                           wsp[:, 2 * t + g, :], start=True, stop=True)
                    mm.then_inc(mix_full, 1)
            for t in range(2):
                for g in range(2):
                    mm = pe.matmul(ps[64 * g:64 * g + 64, 7, t * NS:(t + 1) * NS],
                                   vaT[0:NS, 8, (2 * t + g) * 64:(2 * t + g + 1) * 64],
                                   wss[:, 2 * t + g, :], start=True, stop=True)
            mm.then_inc(mix_full, 1)
            for n in range(18, 20):
                a_tile(n // 2, n % 2, 0, n)

            for br in range(4):
                s = br % 2
                if br == 3:
                    for c in range(NCH):
                        pe.wait_ge(c_conv, 2)
                        for t in range(2):
                            mm = pe.matmul(ps[:, 6, 0:CH], mean256[:], cv[:, t, tokens(c)],
                                           start=(t == 0), stop=(t == 1))
                        mm.then_inc(c_mean, 1)
                        pe.wait_ge(c_sq, c + 1)
                        for t in range(2):
                            mm = pe.matmul(ps[:, 7, 0:CH], mean256[:], csq[:, t, :],
                                           start=(t == 0), stop=(t == 1))
                        mm.then_inc(c_var, 1)
                pe.wait_ge(slot_ready, br + 1)

                def gate_and_branch(p):
                    for j in range(2):
                        a_tile(p, j, first_tile[1] + 8 * br, p * 2 + (N_MIX + 8 * br + j))
                        d_tile(j, p * 2 + (8 * br + j), (8, 9),
                               lambda i, c: slot_hi[:, s, i, tokens(c)],
                               lambda i, c: slot_lo[:, s, i, tokens(c)])

                if br == 0:
                    pe.wait_ge(mix_read, 5)
                    gate_and_branch(0)
                with pe.Fori(1 if br == 0 else 0, KT // 2) as p:
                    gate_and_branch(p)

            pe.wait_ge(m_ready, NCH)
            with pe.Fori(0, KT // 2) as p:
                for j in range(2):
                    pe.wait_ge(w_split, p * 2 + (first_tile[2] + j + 1))
                    d_tile(j, p * 2 + (d_tiles(2) + j), range(8),
                           lambda i, c: h_hi[:, i, tokens(c)], lambda i, c: h_lo[:, i, tokens(c)])
            norm_sums(1)

            for g, size in enumerate(GROUPS):
                if g == 0:
                    for j in range(2):
                        a_tile(0, j, first_tile[UP[0]], normed_tiles(UP[0]) + j, norm=1)
                with pe.Fori(1 if g == 0 else 0, size) as f:
                    for j in range(2):
                        a_tile(f, j, first_tile[UP[g]], f * 2 + (normed_tiles(UP[g]) + j))
                pe.wait_ge(hid_ready, sum(GROUPS[:g + 1]))
                with pe.Fori(0, KT // 2) as p:
                    for j in range(2):
                        pe.wait_ge(w_split, p * 2 + (first_tile[DOWN[g]] + j + 1))
                        d_tile(j, p * 2 + (d_tiles(DOWN[g]) + j), range(size),
                               lambda i, c: hid_hi[:, i, tokens(c)],
                               lambda i, c: hid_lo[:, i, tokens(c)])
            norm_sums(2)

            pe.wait_ge(n_lo, 24 * 3)
            pe.wait_ge(p_ready, 1)
            with pe.Fori(0, KT // 2) as p:
                for j in range(2):
                    a_tile(p, j, first_tile[PLE], p * 2 + (normed_tiles(PLE) + j))
                    d_tile(j, p * 2 + (d_tiles(PLE) + j), (8, 9),
                           lambda i, c: p_hi[:, i, tokens(c)], lambda i, c: p_lo[:, i, tokens(c)])
            norm_sums(3)

        @block.scalar
        def _(act):
            def square_and_round(n, last=False):
                for c in range(NCH):
                    m = NCH * n + c
                    if n == 0:
                        act.wait_ge(x_in[c], 16)
                    elif c == 0:
                        act.wait_ge(*((d_read, 3 * d_tiles(3)), (d_read, 3 * d_tiles(PLE)),
                                      (g_used, 3 * (N_GATE + KT)))[n - 1])
                    for t in range(KT):
                        if t >= 2:
                            act.wait_ge(n_add, 7 * m + max(1, t - 2))
                        elif m > 0:
                            act.wait_ge(n_add, 7 * m)
                        act.activation(sq[:, t % 2, :], X[:, t, tokens(c)], ACT.Square
                                       ).then_inc(n_sq, 1)
                    act.wait_ge(n_sum, m + 1)
                    if m >= 2:
                        act.wait_ge(n_t, 8 * (m - 1))
                    act.activation(rstd[:, m % 2, :], ps[:, 6 + m % 2, 0:CH], ACT.Sqrt,
                                   bias=eps_col).then_inc(n_std, 1)
                    if not last:
                        for t in range(KT):
                            act.wait_ge(n_t, 8 * m + t + 1)
                            act.activation(h_hi[:, t, tokens(c)], nt[:, t % 2, :], ACT.Copy
                                           ).then_inc(n_hi, 1)
                    else:
                        for t in range(KT):
                            act.wait_ge(n_t, 8 * m + t + 1)
                            i = KT * c + t
                            act.dma_start(d["y"][t, :, tokens(c)], nt[:, t % 4, :]
                                          ).then_inc(out_y[i % 4], 16)

            def evacuate(a, dst, func=ACT.Copy, **kw):
                for c in range(NCH):
                    act.wait_ge(a_full, a * 3 + (c + 1))
                    act.activation(dst[:, tokens(c)], ps[:, c, 0:CH], func, **kw
                                   ).then_inc(a_read, 1)

            def evacuate_padded(a, dst, pad):
                for c in range(NCH):
                    act.wait_ge(a_full, a * 3 + (c + 1))
                    if c < NCH - 1:
                        act.activation(dst[:, pad + c * CH:pad + (c + 1) * CH], ps[:, c, 0:CH],
                                       ACT.Copy).then_inc(a_read, 1)
                    else:
                        act.activation(dst[:, pad + c * CH:pad + TP], ps[:, c, 0:PC], ACT.Copy)
                        act.activation(sample_cols(dst, pad), as_samples(ps[:, c, PC:CH]),
                                       ACT.Copy).then_inc(a_read, 1)

            act.wait_ge(consts_in, 16 * 6)
            square_and_round(0)
            for n, dst in enumerate((q, q, k, k, v, v)):
                evacuate(n, dst[:, n % 2, :])
            act.wait_ge(a_read, 18)
            act.dma_start(d["k_out"], k[:]).then_inc(out_kv, 16)
            act.dma_start(d["v_out"], v[:]).then_inc(out_kv, 16)

            def softplus_part(i):
                w, n = width(i), keys(i)
                act.wait_ge(z_read, i + 1)
                if i >= 2:
                    act.wait_ge(sp_ready, i - 1)
                act.activation(le[0:n, i % 2, w], zb[0:n, i % 4, w], ACT.Abs).then_inc(lch, 1)
                act.wait_ge(lch, 2 * i + 1)
                act.activation(le[0:n, i % 2, w], le[0:n, i % 2, w], ACT.Exp, scale=-1.0
                               ).then_inc(lch, 1)
                act.wait_ge(lch, 2 * i + 2)
                act.activation(le[0:n, i % 2, w], le[0:n, i % 2, w], ACT.Ln, bias=one_col[0:n]
                               ).then_inc(l_ready, 1)

            def weights_of(i):
                w, n = width(i), keys(i)
                act.wait_ge(t_ready, i + 1)
                if i >= 3:
                    act.wait_ge(pv_done, i - 2)
                act.activation(av[0:n, i % 3, w], zb[0:n, i % 4, w], ACT.Exp).then_inc(a_ready, 1)

            softplus_part(0)
            for i in range(STEPS + 1):
                if i + 1 < STEPS:
                    softplus_part(i + 1)
                if i >= 1:
                    weights_of(i - 1)

            act.wait_ge(slot_ready, 1)
            act.wait_ge(out_kv, 16 * 2)
            for n in range(6, 8):
                evacuate(n, va[:, n % 2, :], ACT.Gelu_apprx_tanh)
            for n in range(8, 10):
                evacuate(n, u[:, n % 2, :], ACT.Gelu_apprx_tanh)
            act.wait_ge(pads_ready, 4)
            for t in range(2):
                evacuate_padded(10 + 2 * t, pb[:, t, :], 2)
                evacuate(11 + 2 * t, side[:, t, :])
            for t in range(2):
                evacuate_padded(14 + 2 * t, pcv[:, t, :], CW - 1)
                act.wait_ge(prod_done, t + 1)
                evacuate(15 + 2 * t, side[:, t, :], ACT.Sigmoid)
            for t in range(2):
                act.wait_ge(prod_done, t + 1)
                act.dma_start(d["b_last"][t], last_cols(pb[:, t, :], 2)).then_inc(out_state, 16)
            for t in range(2):
                act.wait_ge(prod_done, t + 3)
                act.dma_start(d["c_last"][t], last_cols(pcv[:, t, :], CW - 1)
                              ).then_inc(out_state, 16)
            act.wait_ge(va_stat, 9)
            act.activation(stat[:, 0:8, 4:5], stat[:, 0:8, 7:8], ACT.Sqrt, bias=eps_col)
            act.activation(stat[0:NS, 8:9, 4:5], stat[0:NS, 8:9, 7:8], ACT.Sqrt,
                           bias=eps_col[0:NS]).then_inc(va_std, 1)
            act.wait_ge(va_done, 9)
            act.dma_start(d["va_out"], vaT[0:NS, 8, :]).then_inc(out_va, 16)
            act.wait_ge(slot_ready, 2)
            for n in range(18, 20):
                evacuate(n, bg[:, n % 2, :])

            def gates(p, j, a, used):
                for c in range(NCH):
                    act.wait_ge(a_full, p * 6 + ((a + j) * 3 + c + 1))
                    if not (isinstance(p, int) and p == 0 and used + j == 0):
                        act.wait_ge(g_used, p * 6 + ((used + j) * 3 + c - 2))
                    act.activation(gate[:, c, :], ps[:, c, 0:CH], ACT.Sigmoid).then_inc(a_read, 1)

            act.wait_ge(out_va, 16)
            for br in range(4):
                if br == 3:
                    for c in range(NCH):
                        act.wait_ge(c_cent, c + 1)
                        act.activation(csq[:], cv[:, :, tokens(c)], ACT.Square).then_inc(c_sq, 1)
                        act.wait_ge(c_var, c + 1)
                        if c:
                            act.wait_ge(c_norm, c)
                        act.activation(cstd[:], ps[:, 7, 0:CH], ACT.Sqrt, bias=eps_col
                                       ).then_inc(c_std, 1)
                    act.wait_ge(c_norm, NCH)
                    for t in range(2):
                        act.activation(cv[:, t, :], cv[:, t, :], ACT.Silu, scale=ln_c[:, t:t + 1],
                                       bias=ln_c[:, 2 + t:3 + t]).then_inc(c_act, 1)
                if br == 0:
                    for j in range(2):
                        gates(0, j, N_MIX, 0)
                with act.Fori(1 if br == 0 else 0, KT // 2) as p:
                    for j in range(2):
                        gates(p, j, N_MIX + 8 * br, 8 * br)

            square_and_round(1)

            def up_tile(f, j, a, tile):
                buf = up[:, j, :]
                act.wait_ge(up_used, f * 2 + (tile + j + 1))
                act.activation(sample_states(buf, 2), as_samples(
                    ffn_state[:, bass.ds(f * 2 + (tile + j), 1), :].rearrange("p a n -> p (a n)")),
                    ACT.Copy)
                evacuate_padded(f * 2 + (a + j), buf, 2)

            f0 = 0
            for g, size in enumerate(GROUPS):
                with act.Fori(0, size) as f:
                    up_tile(f, 0, normed_tiles(UP[g]), 2 * f0)
                    up_tile(f, 1, normed_tiles(UP[g]), 2 * f0)
                    act.wait_ge(up_used, f * 2 + (2 * f0 + 3))
                    act.activation(cu[:, 0, :], cu[:, 0, :], ACT.Silu).then_inc(ga_act, 1)
                    act.wait_ge(prod_ready, f + (f0 + 1))
                    act.activation(hid_hi[:, bass.ds(f, 1), 0:TP].rearrange("p a n -> p (a n)"),
                                   cu[:, 1, 0:TP], ACT.Copy)
                    act.activation(as_samples(hid_hi[:, bass.ds(f, 1), TP:T]
                                              .rearrange("p a n -> p (a n)")),
                                   cu[:, 1, TP:].rearrange("p (b t) -> p b t", b=NB)[:, :, 2:],
                                   ACT.Copy).then_inc(hid_h, 1)
                f0 += size
            act.wait_ge(up_used, 2 * FT + 2)
            act.dma_start(d["ffn_last"], ffn_last[:]).then_inc(out_last, 16)
            square_and_round(2)
            with act.Fori(0, KT // 2) as p:
                for j in range(2):
                    gates(p, j, normed_tiles(PLE), N_GATE)
            square_and_round(3, last=True)
            for n in range(4):
                act.wait_ge(out_y[n], 16 * 6)
            act.wait_ge(out_last, 16)

        @block.vector
        def _(dve):
            chain = [0]

            def link(ins):
                ins.then_inc(dch, 1)
                chain[0] = chain[0] + 1
                dve.wait_ge(dch, chain[0])

            class Loop:

                def __init__(self, start, end, per):
                    self.start, self.end, self.per = start, end, per

                def __enter__(self):
                    self.before = chain[0]
                    self.loop = dve.Fori(self.start, self.end)
                    i = self.loop.__enter__()
                    chain[0] = (i - self.start) * self.per + self.before if self.start else \
                        i * self.per + self.before
                    return i

                def __exit__(self, *a):
                    self.loop.__exit__(*a)
                    chain[0] = self.before + (self.end - self.start) * self.per

            def norm(n, gains, last=False):
                for c in range(NCH):
                    m = NCH * n + c
                    for t in range(1, KT):
                        dve.wait_ge(n_sq, 8 * m + t + 1)
                        if t == 1:
                            dve.tensor_tensor(ssum[:, m % 2, :], sq[:, 0, :], sq[:, 1, :], ALU.add
                                              ).then_inc(n_add, 1)
                        else:
                            dve.wait_ge(n_add, 7 * m + t - 1)
                            dve.tensor_tensor(ssum[:, m % 2, :], ssum[:, m % 2, :],
                                              sq[:, t % 2, :], ALU.add).then_inc(n_add, 1)
                    dve.wait_ge(n_std, m + 1)
                    link(dve.reciprocal(rstd[:, m % 2, :], rstd[:, m % 2, :]))

                    def low(t):
                        dve.wait_ge(n_hi, 8 * m + t + 1)
                        dve.tensor_tensor(h_lo[:, t, tokens(c)], nt[:, t % 2, :],
                                          h_hi[:, t, tokens(c)], ALU.subtract).then_inc(n_lo, 1)

                    for t in range(KT):
                        if not last:
                            if t >= 2:
                                low(t - 2)
                                dve.wait_ge(n_lo, 8 * m + t - 1)
                            elif m > 0:
                                dve.wait_ge(n_lo, 8 * m)
                        else:
                            i = KT * c + t
                            if i >= 4:
                                dve.wait_ge(out_y[i % 4], 16 * (i // 4))
                        dve.scalar_tensor_tensor(out=nt[:, t % (4 if last else 2), :],
                                                 in0=X[:, t, tokens(c)], scalar=gains[:, t:t + 1],
                                                 in1=rstd[:, m % 2, :], op0=ALU.mult, op1=ALU.mult
                                                 ).then_inc(n_t, 1)
                    if not last:
                        low(KT - 2)
                        low(KT - 1)

            dve.wait_ge(consts_in, 16 * 6)
            norm(0, g_cols["mix"])

            def transposed(dst, n0):
                for blk in range(9):
                    w_ = P if blk < 8 else NS
                    n = n0 + blk
                    dve.wait_ge(tr_full, n + 1)
                    dve.tensor_copy(dst[0:w_, blk, :], ps[0:w_, 6 + n % 2, 0:W]
                                    ).then_inc(tr_read, 1)

            dve.wait_ge(att_in, 16 * 6)
            link(dve.memset(qbd[:], 0.0))
            dve.wait_ge(a_read, 18)
            for hp in range(2):
                for h2 in range(2):
                    r = slice(64 * h2, 64 * h2 + 64)
                    ins = dve.tensor_copy(qbd[r, hp, :, h2, :], as_samples(q[r, hp, TP:T]))
            ins.then_inc(qbd_ready, 1)
            transposed(vT, 0)
            dve.wait_ge(tr_read, 9)

            def biased(i):
                w, n = width(i), keys(i)
                dve.wait_ge(z_full, i + 1)
                if i >= 4:
                    dve.wait_ge(a_ready, i - 3)
                src, out = ps[0:n, 5 + i % 2, w], zb[0:n, i % 4, w]
                if i < NU:
                    h = units[i][0]
                    dve.tensor_scalar(out, src, HD ** -0.5, sb_bias[:, h:h + 1], ALU.mult, ALU.add
                                      ).then_inc(z_read, 1)
                else:
                    dve.scalar_tensor_tensor(out=out, in0=src, scalar=HD ** -0.5, in1=bcol[0:n, :],
                                             op0=ALU.mult, op1=ALU.add).then_inc(z_read, 1)

            def exponent(i):
                w, n = width(i), keys(i)
                dve.wait_ge(later_full, i + 1)
                z = zb[0:n, i % 4, w]
                bank = 3 + units[i][0] % 2 if i < NU else 3
                dve.wait_ge(z_read, i + 1)
                ins = dve.tensor_tensor(z, z, ps[0:n, bank, w], ALU.subtract)
                if on_diagonal(i):
                    link(ins)
                    m = zb[0:n, i % 4, offset(i) if i < NU else 0:][:, 0:P]
                    ins = dve.tensor_tensor(m, m, (causal if i < NU else own)[0:n, 1, :], ALU.add)
                ins.then_inc(t_ready, 1)

            def softplus(i):
                w, n = width(i), keys(i)
                dve.wait_ge(l_ready, i + 1)
                if i >= 2:
                    dve.wait_ge(later_full, i)
                ins = dve.scalar_tensor_tensor(out=spl[0:n, i % 2, w], in0=zb[0:n, i % 4, w],
                                               scalar=0.0, in1=le[0:n, i % 2, w], op0=ALU.max,
                                               op1=ALU.add)
                if on_diagonal(i):
                    link(ins)
                    m = spl[0:n, i % 2, offset(i) if i < NU else 0:][:, 0:P]
                    ins = dve.tensor_tensor(m, m, (causal if i < NU else own)[0:n, 0, :], ALU.mult)
                ins.then_inc(sp_ready, 1)

            def output(i):
                dve.wait_ge(pv_done, i + 1)
                if i < NU:
                    h, qc, _ = units[i]
                    r = slice(HD * (h % 2), HD * (h % 2) + HD)
                    dve.tensor_copy(q[r, h // 2, qc * QC:(qc + 1) * QC], ps[r, 7, :]
                                    ).then_inc(o_read, 1)
                else:
                    for hp in range(2):
                        for h2 in range(2):
                            r = slice(64 * h2, 64 * h2 + 64)
                            src = ps[r, 7, hp * 64:(hp + 1) * 64].rearrange(
                                "p (b h t) -> p b h t", b=NB, h=2)[:, :, h2, :]
                            ins = dve.tensor_copy(as_samples(q[r, hp, TP:T]), src)
                    ins.then_inc(o_read, 1)

            biased(0)
            for i in range(STEPS + 3):
                if i >= 3 and is_last(i - 3):
                    output(i - 3)
                if i + 1 < STEPS:
                    biased(i + 1)
                if 1 <= i <= STEPS:
                    exponent(i - 1)
                if i < STEPS:
                    softplus(i)

            def into_slot(s, src):
                link(dve.tensor_copy(slot_hi[:, s], src))
                dve.tensor_tensor(slot_lo[:, s], src, slot_hi[:, s], ALU.subtract
                                  ).then_inc(slot_ready, 1)

            dve.wait_ge(o_read, chains_before(STEPS))
            into_slot(0, q[:])

            for t in range(2):
                dve.memset(pb[:, t, 0:2], 0.0).then_inc(pads_ready, 1)
                dve.memset(pcv[:, t, 0:CW - 1], 0.0).then_inc(pads_ready, 1)

            def times_side(n, buf, pad, t):
                dve.wait_ge(a_read, 3 * (n + 1))
                dve.tensor_tensor(buf[:, pad:pad + TP], buf[:, pad:pad + TP], side[:, t, 0:TP],
                                  ALU.mult)
                dve.tensor_tensor(sample_cols(buf, pad), sample_cols(buf, pad),
                                  as_samples(side[:, t, TP:T]), ALU.mult).then_inc(prod_done, 1)

            dve.wait_ge(mixc_in, 16 * 9)
            for t in range(2):
                times_side(11 + 2 * t, pb[:, t, :], 2, t)
            for t in range(2):
                times_side(15 + 2 * t, pcv[:, t, :], CW - 1, t)

            transposed(vaT, 9)
            for blk in range(9):
                n = P if blk < 8 else NS
                dve.wait_ge(tr_read, 9 + blk + 1)
                link(dve.bn_stats(stat[0:n, blk, 0:6], vaT[0:n, blk, :]))
                dve.bn_aggr(stat[0:n, blk, 6:8], stat[0:n, blk, 0:6]).then_inc(va_stat, 1)
            dve.wait_ge(va_std, 1)
            for blk in range(9):
                n = P if blk < 8 else NS
                link(dve.reciprocal(stat[0:n, blk, 4:5], stat[0:n, blk, 4:5]))
                link(dve.tensor_scalar(vaT[0:n, blk, :], vaT[0:n, blk, :], stat[0:n, blk, 6:7],
                                       stat[0:n, blk, 4:5], ALU.subtract, ALU.mult))
                link(dve.tensor_tensor(vaT[0:n, blk, :], vaT[0:n, blk, :], lnv[0:n, 0, :], ALU.mult))
                dve.tensor_tensor(vaT[0:n, blk, :], vaT[0:n, blk, :], lnv[0:n, 1, :], ALU.add
                                  ).then_inc(va_done, 1)
            for t in range(2):
                for half in range(2):
                    bank = 3 + 2 * t + half
                    part = slice(half * 512, (half + 1) * 512)
                    dve.wait_ge(mix_full, 2 * t + half + 1)
                    ins = dve.tensor_tensor(
                        side[:, t, part].rearrange("p (c n) -> p c n", c=4),
                        ps[:, bank, :].rearrange("p (c n) -> p c n", c=4),
                        bsp[:, t, :].rearrange("p (c n) -> p c n", c=1).to_broadcast([P, 4, P]), ALU.add)
                    ins.then_inc(mix_read, 1)
                    dve.wait_ge(mix_read, bank - 2)
                    link(dve.tensor_tensor(u[:, t, part], u[:, t, part], side[:, t, part], ALU.mult))
            dve.wait_ge(mix_full, 5)
            dve.tensor_tensor(side[:, :, TP:T], ps[:, 7, 0:2 * NS].rearrange("p (t n) -> p t n", t=2),
                              bss[:], ALU.add).then_inc(mix_read, 1)
            dve.wait_ge(mix_read, 5)
            link(dve.tensor_tensor(u[:, :, TP:T], u[:, :, TP:T], side[:, :, TP:T], ALU.mult))
            into_slot(1, u[:])

            def merge(p, j, a, dn, first):
                m = bass.ds(p * 2 + j, 1)
                for c in range(NCH):
                    dve.wait_ge(a_read, p * 6 + ((a + j) * 3 + c + 1))
                    dve.wait_ge(d_full, p * 6 + ((dn + j) * 3 + c + 1))
                    g = gate[:, c, :]
                    dve.tensor_tensor(g, g, ps[:, 3 + c, 0:CH], ALU.mult).then_inc(d_read, 1)
                    x = X[:, m, tokens(c)].rearrange("p a n -> p (a n)")
                    dve.wait_ge(d_read, p * 6 + ((dn + j) * 3 + c + 1))
                    if first:
                        dve.tensor_copy(x, g).then_inc(g_used, 1)
                    else:
                        dve.tensor_tensor(x, x, g, ALU.add).then_inc(g_used, 1)

            def taps(src, out_w, w, k0, k1):
                out = acc[:, 0:out_w]
                for i in range(k0, k1):
                    x = src[:, i:i + out_w]
                    if i == 0:
                        link(dve.tensor_scalar(out, x, w[:, 0:1], None, ALU.mult))
                    else:
                        link(dve.scalar_tensor_tensor(out=out, in0=x, scalar=w[:, i:i + 1], in1=out,
                                                      op0=ALU.mult, op1=ALU.add))

            def conv_b(t):
                def run():
                    n = LB - 2
                    if t == 0:
                        dve.wait_ge(a_read, 3 * 20)
                    taps(pb[:, t, :], n, conv_b_w[:, 3 * t:3 * t + 3], 0, 3)
                    link(dve.tensor_tensor(bg[:, t, 0:TP], bg[:, t, 0:TP], acc[:, 0:TP], ALU.mult))
                    link(dve.tensor_tensor(
                        as_samples(bg[:, t, TP:T]), as_samples(bg[:, t, TP:T]),
                        acc[:, TP:n].rearrange("p (b t) -> p b t", b=NB)[:, :, 2:], ALU.mult))
                return run

            def conv_c(t, k0, k1):
                def run():
                    n = LC - CW + 1
                    taps(pcv[:, t, :], n, conv_c_w[:, CW * t:CW * (t + 1)], k0, k1)
                    if k1 == CW:
                        if t == 0:
                            dve.wait_ge(out_state, 16 * 4)
                        link(dve.tensor_copy(cv[:, t, 0:TP], acc[:, 0:TP]))
                        ins = dve.tensor_copy(
                            as_samples(cv[:, t, TP:T]),
                            acc[:, TP:n].rearrange("p (b t) -> p b t", b=NB)[:, :, CW - 1:])
                        ins.then_inc(c_conv, 1)
                        dve.wait_ge(c_conv, t + 1)
                return run

            def several(fs):
                def run():
                    for f in fs:
                        f()
                return run

            steps = [conv_b(0), conv_b(1)]
            cuts = [0, 5, 10, 15, 20, 25, CW]
            for t in range(2):
                steps += [conv_c(t, a, b) for a, b in zip(cuts, cuts[1:])]
            steps += [lambda: None] * (16 - len(steps))
            for br in range(4):
                a, dn = N_MIX + 8 * br, 8 * br
                if br == 2:
                    into_slot(0, bg[:])
                if br == 3:
                    for c in range(NCH):
                        dve.wait_ge(c_mean, c + 1)
                        for t in range(2):
                            ins = dve.tensor_tensor(cv[:, t, tokens(c)], cv[:, t, tokens(c)],
                                                    ps[:, 6, 0:CH], ALU.subtract)
                        ins.then_inc(c_cent, 1)
                        dve.wait_ge(c_cent, c + 1)
                        dve.wait_ge(c_std, c + 1)
                        link(dve.reciprocal(cstd[:], cstd[:]))
                        for t in range(2):
                            ins = dve.tensor_tensor(cv[:, t, tokens(c)], cv[:, t, tokens(c)],
                                                    cstd[:], ALU.mult)
                        ins.then_inc(c_norm, 1)
                        dve.wait_ge(c_norm, c + 1)
                    dve.wait_ge(c_act, 2)
                    into_slot(1, cv[:])
                if br < 2:
                    for m in range(KT):
                        merge(m // 2, m % 2, a, dn, br == 0)
                        steps[8 * br + m]()
                else:
                    with dve.Fori(0, KT // 2) as p:
                        for j in range(2):
                            merge(p, j, a, dn, False)
            dve.wait_ge(g_used, 3 * N_GATE)
            for c in range(NCH):
                link(dve.tensor_copy(h_hi[:, :, tokens(c)], X[:, :, tokens(c)]))
                dve.tensor_tensor(h_lo[:, :, tokens(c)], X[:, :, tokens(c)], h_hi[:, :, tokens(c)],
                                  ALU.subtract).then_inc(m_ready, 1)
            dve.wait_ge(m_ready, NCH)

            dve.wait_ge(x2_in, 16 * 3)
            nd = d_tiles(2)
            with dve.Fori(0, KT // 2) as p:
                for j in range(2):
                    m = bass.ds(p * 2 + j, 1)
                    for c in range(NCH):
                        dve.wait_ge(d_full, p * 6 + (nd + j) * 3 + (c + 1))
                        dve.tensor_tensor(X[:, m, tokens(c)].rearrange("p a n -> p (a n)"),
                                          x_again[:, m, tokens(c)].rearrange("p a n -> p (a n)"),
                                          ps[:, 3 + c, 0:CH], ALU.add).then_inc(d_read, 1)
            dve.wait_ge(d_read, 3 * (nd + KT))
            dve.memset(up[:, 0, 0:2], 0.0).then_inc(up_used, 1)
            dve.memset(up[:, 1, 0:2], 0.0).then_inc(up_used, 1)
            norm(1, g_cols["ffn"])

            def convolve(f, j, a, tile):
                one = bass.ds(f * 2 + (tile + j), 1)
                dve.wait_ge(a_read, f * 6 + (a + j) * 3 + 3)
                n = LB - 2
                out, x = cu[:, j, :], up[:, j, :]
                w = ffn_w[:, one, :].rearrange("p a n -> p (a n)")
                dve.tensor_copy(ffn_last[:, one, :].rearrange("p a (b t) -> p (a b) t", t=2),
                                last_cols(x, 2))
                link(dve.tensor_scalar(out, x[:, 0:n], w[:, 0:1], None, ALU.mult))
                link(dve.scalar_tensor_tensor(out=out, in0=x[:, 1:1 + n], scalar=w[:, 1:2], in1=out,
                                              op0=ALU.mult, op1=ALU.add))
                dve.scalar_tensor_tensor(out=out, in0=x[:, 2:2 + n], scalar=w[:, 2:3], in1=out,
                                         op0=ALU.mult, op1=ALU.add).then_inc(up_used, 1)

            f0 = 0
            for g, size in enumerate(GROUPS):
                with Loop(0, size, 4) as f:
                    convolve(f, 0, normed_tiles(UP[g]), 2 * f0)
                    convolve(f, 1, normed_tiles(UP[g]), 2 * f0)
                    dve.wait_ge(up_used, f * 2 + (2 * f0 + 4))
                    dve.wait_ge(ga_act, f + (f0 + 1))
                    dve.tensor_tensor(cu[:, 1, :], cu[:, 1, :], cu[:, 0, :], ALU.mult
                                      ).then_inc(prod_ready, 1)
                    dve.wait_ge(hid_h, f + (f0 + 1))
                    one = bass.ds(f, 1)
                    dve.tensor_tensor(hid_lo[:, one, 0:TP].rearrange("p a n -> p (a n)"),
                                      cu[:, 1, 0:TP],
                                      hid_hi[:, one, 0:TP].rearrange("p a n -> p (a n)"),
                                      ALU.subtract)
                    dve.tensor_tensor(
                        as_samples(hid_lo[:, one, TP:T].rearrange("p a n -> p (a n)")),
                        cu[:, 1, TP:].rearrange("p (b t) -> p b t", b=NB)[:, :, 2:],
                        as_samples(hid_hi[:, one, TP:T].rearrange("p a n -> p (a n)")),
                        ALU.subtract).then_inc(hid_ready, 1)
                f0 += size
                nd = d_tiles(DOWN[g])
                with dve.Fori(0, KT // 2) as p:
                    for j in range(2):
                        m = bass.ds(p * 2 + j, 1)
                        for c in range(NCH):
                            dve.wait_ge(d_full, p * 6 + (nd + j) * 3 + (c + 1))
                            x = X[:, m, tokens(c)].rearrange("p a n -> p (a n)")
                            dve.tensor_tensor(x, x, ps[:, 3 + c, 0:CH], ALU.add
                                              ).then_inc(d_read, 1)
                dve.wait_ge(d_read, 3 * (nd + KT))
            norm(2, g_cols["ple"])

            dve.wait_ge(p_land, 16)
            link(dve.tensor_copy(p_hi[:], p_in[:]))
            dve.tensor_tensor(p_lo[:], p_in[:], p_hi[:], ALU.subtract).then_inc(p_ready, 1)
            with dve.Fori(0, KT // 2) as p:
                for j in range(2):
                    merge(p, j, normed_tiles(PLE), d_tiles(PLE), False)
            dve.wait_ge(g_used, 3 * (N_GATE + KT))
            norm(3, g_cols["final"], last=True)


def tiles(w, n0, n1):
    kt = w.shape[0] // P
    return w[:, n0:n1].reshape(kt, P, (n1 - n0) // P, P).transpose(2, 1, 0, 3)


def feature_major(a, n):
    return a.reshape(-1, n, P).transpose(2, 1, 0)


def layout(i):
    f = np.float32
    w_in, w_br, w_up, w_down = i["w_in"][0], i["w_br"][0], i["w_up"][0], i["w_down"][0]
    a0, b0, c0, d0, g0 = 0, 512, 1280, 1792, 2560
    mix = [(d0, 6), (a0 + 256, 2), (a0, 2)]
    mix += [(b0 + 256, 1), (b0 + 512, 1), (b0 + 384, 1), (b0 + 640, 1)]
    mix += [(c0, 1), (c0 + 256, 1), (c0 + 128, 1), (c0 + 384, 1), (b0, 2)]
    w_mix = np.concatenate([tiles(w_in, o, o + n * P) for o, n in mix])
    gates = []
    for br in (3, 0, 1, 2):
        o = g0 + br * D_MODEL
        gates.append(np.concatenate([tiles(w_in, o, o + D_MODEL), tiles(w_br[br], 0, D_MODEL)], axis=2))
    w_upt = np.stack([tiles(w_up, 0, D_FF), tiles(w_up, D_FF, 2 * D_FF)], axis=1)
    downs = np.zeros((len(GROUPS) * KT, P, 6, P), f)
    f0 = 0
    for n, g in enumerate(GROUPS):
        downs[n * KT:(n + 1) * KT, :, :g] = tiles(w_down[f0 * P:(f0 + g) * P], 0, D_MODEL)
        f0 += g
    w_ple = np.concatenate([tiles(i["w_ple_gate"][0], 0, D_MODEL), tiles(i["w_ple"][0], 0, D_MODEL)],
                           axis=2)
    flat = lambda a: np.ascontiguousarray(a).reshape(a.shape[0], P, -1)
    x = np.concatenate([i["x_prompt"].reshape(TP, D_MODEL), i["x_sample"].reshape(NS, D_MODEL)])
    p = np.concatenate([i["p_prompt"].reshape(TP, W), i["p_sample"].reshape(NS, W)])
    x = feature_major(x, KT).reshape(P, KT, NCH, CH).transpose(2, 0, 1, 3)
    small = np.zeros((P, 256), f)
    for n, g in enumerate(("g_mix", "g_ffn", "g_ple", "g_final")):
        small[:, 8 * n:8 * n + 8] = i[g].reshape(KT, P).T
    small[:, 32] = EPS
    small[:, 33:37] = i["sb_bias"][0]
    small[:, 37:39] = i["ln_c_g"][0].reshape(2, P).T
    small[:, 39:41] = i["ln_c_b"][0].reshape(2, P).T
    small[:, 41:47] = i["conv_b_w"][0].reshape(3, 2, P).transpose(2, 1, 0).reshape(P, 6)
    small[:, 47:47 + 2 * CW] = i["conv_c_w"][0].reshape(CW, 2, P).transpose(2, 1, 0).reshape(P, -1)
    small[:, 110] = 1.0
    ffn_w = i["ffn_conv_w"][0].reshape(3, 2, FT, P).transpose(3, 2, 1, 0).reshape(P, 2 * FT, 3)
    ffn_state = i["state_ffn_conv"][0].reshape(NB, 2, 2, FT, P).transpose(4, 3, 2, 0, 1)
    k_, q_ = np.arange(P)[:, None], np.arange(P)[None, :]
    later = (q_ > k_).astype(f)
    causal = np.stack([later, np.where(q_ > k_, 0, NEG).astype(f)], axis=1)
    col = np.arange(P)
    cb, ct = (col // 8) % NB, col % TS
    kb, kt_ = np.arange(NS)[:, None] // TS, np.arange(NS)[:, None] % TS
    ok = (kb == cb[None]) & (kt_ < ct[None])
    own = np.zeros((P, 2, P), f)
    own[:NS, 0] = ok
    own[:NS, 1] = np.where(ok, 0, NEG)
    bias = i["sb_bias"][0].reshape(2, 1, 2, 1)
    bcol = np.broadcast_to(np.broadcast_to(bias, (2, NB, 2, TS)).reshape(1, P), (P, P))
    lnv = np.stack([np.broadcast_to(i[n][0], (P, W)) for n in ("ln_v_g", "ln_v_b")], axis=1)
    w_sp, b_sp = i["w_sp"][0], i["b_sp"][0]
    bsp = np.broadcast_to(b_sp.reshape(2, 2, 1, P), (2, 2, 64, P)).reshape(2, P, P).transpose(1, 0, 2)
    bss = np.broadcast_to(bsp[:, :, None, :TS], (P, 2, NB, TS)).reshape(P, 2, NS)
    wss = np.zeros((NB, TS, 4, NB, TS), f)
    for b in range(NB):
        wss[b, :, :, b, :] = w_sp[:, :TS, :TS].transpose(2, 0, 1)
    out = dict(
        x=x, p=feature_major(p, 2), small=small, ident=np.eye(P, dtype=f),
        mean1024=np.full((P, P), 1 / D_MODEL, f), mean256=np.full((P, P), 1 / W, f),
        ffn_w=ffn_w, ffn_state=ffn_state.reshape(P, 2 * FT, 2 * NB),
        tri=(k_ >= q_).astype(f), comp=(k_ < q_).astype(f), causal=causal, own=own, bcol=bcol,
        ptab=i["page_table"].reshape(1, -1).astype(np.int32),
        cache_kT=i["cache_k"][0].reshape(N_PHYS, P, 2, P).transpose(0, 3, 2, 1).reshape(N_PHYS, P, W),
        cache_v=i["cache_v"][0].reshape(N_PHYS, P, W),
        state_b=i["state_conv_b"][0].reshape(NB, 2, 2, P).transpose(2, 3, 0, 1),
        state_c=i["state_conv_c"][0].reshape(NB, CW - 1, 2, P).transpose(2, 3, 0, 1),
        lnv=lnv, wsp=w_sp.transpose(2, 0, 1), bsp=bsp, bss=bss, wss=wss.reshape(NS, 4, NS),
        w_mix=flat(w_mix), w_gate=flat(np.concatenate(gates)), w_o=flat(tiles(i["w_o"][0], 0, D_MODEL)),
        w_up=flat(w_upt.reshape(2 * FT, P, KT, P)), w_down=flat(downs), w_ple=flat(w_ple))
    return {n: np.ascontiguousarray(a) for n, a in out.items()}


OUTS = dict(y=(KT, P, T), k_out=(P, 2, T), v_out=(P, 2, T), va_out=(NS, W), b_last=(2, P, NB + 1, 2),
            c_last=(2, P, NB + 1, CW - 1), ffn_last=(P, 2 * FT, 2 * (NB + 1)))


def kernel(**inputs):
    import concourse.bacc as bacc
    from concourse.bass_utils import run_bass_kernel_spmd

    nc = bacc.Bacc("TRN2", target_bir_lowering=False, num_devices=1)
    arrays = layout({n: np.asarray(a) for n, a in inputs.items()})
    d = {n: nc.dram_tensor(n + "_dram", a.shape, mybir.dt.from_np(a.dtype), kind="ExternalInput").ap()
         for n, a in arrays.items()}
    for n, shape in OUTS.items():
        d[n] = nc.dram_tensor(n + "_dram", shape, F32, kind="ExternalOutput").ap()
    hybrid_layer(nc, d)
    r = run_bass_kernel_spmd(nc, [{n + "_dram": a for n, a in arrays.items()}], core_ids=[0]).results[0]
    r = {n: np.asarray(r[n + "_dram"]) for n in OUTS}
    y = r["y"].reshape(D_MODEL, T).T
    kv = [r[n].transpose(2, 1, 0).reshape(T, HEADS, HD) for n in ("k_out", "v_out")]
    new = [a[:TP].reshape(1, 1, TP, HEADS, HD) for a in kv]
    new += [a[TP:].reshape(1, NB, TS, HEADS, HD) for a in kv]
    last_b = r["b_last"].transpose(2, 3, 0, 1).reshape(NB + 1, 2, W)
    last_c = r["c_last"].transpose(2, 3, 0, 1).reshape(NB + 1, CW - 1, W)
    last_f = r["ffn_last"].reshape(P, FT, 2, NB + 1, 2).transpose(3, 4, 2, 1, 0).reshape(NB + 1, 2, -1)
    states = [last_b, last_c, last_f]
    out = [y[:TP].reshape(1, TP, D_MODEL), y[TP:].reshape(NB, TS, D_MODEL), new[0], new[1]]
    out += [s[None, :1] for s in states]
    out += [new[2], new[3], r["va_out"].reshape(1, NB, TS, W)]
    out += [s[None, 1:] for s in states]
    return tuple(np.ascontiguousarray(a) for a in out)
```

```python
from contextlib import ExitStack

import numpy as np

import concourse.bass as bass
from concourse import mybir

F32 = mybir.dt.float32
F32R = mybir.dt.float32r
I32 = mybir.dt.int32
ALU = mybir.AluOpType
ACT = mybir.ActivationFunctionType

P = 128
D_MODEL = 1024
KT = D_MODEL // P
TP = 1024
NB, TS = 8, 4
NS = NB * TS
T = TP + NS
CH = T // 3
NCH = 3
PC = TP - 2 * CH
W = 256
HEADS, HD = 4, 64
D_FF = 2816
FT = D_FF // P
GROUPS = (5, 5, 4, 4, 4)
UPS = (6, 5, 4, 4, 3)
AHEAD = (0, 5, 4, 5, 4)
N_PAGES, PAGE = 8, 128
N_PHYS = 80
EPS = 1e-6
N_MIX = 20
N_GATE = 32
QC = 512
NEG = -1.0e30
CW = 31
LB = 2 + TP + NB * (2 + TS)
LC = (CW - 1) + TP + NB * (CW - 1 + TS)


def units_of_prompt():
    out = []
    for pair in range(HEADS // 2):
        for qc in range(TP // QC):
            for kb in reversed(range((qc + 1) * QC // P)):
                for half in range(2):
                    out.append((2 * pair + half, qc, kb))
    return out


def hybrid_layer(nc, d):
    units = units_of_prompt()
    NU = len(units)
    STEPS = NU + 1 + N_PAGES
    ctx = ExitStack()
    with ctx:
        def sem(name):
            return ctx.enter_context(nc.semaphore(name))

        base = 16512

        def at(name, shape, dt, offset):
            size = int(np.prod(shape[1:])) * 4
            assert offset % 32 == 0 and base + offset + size <= 229344, (name, offset, size)
            return nc.alloc_sbuf_tensor_at(name, shape, dt, offset=base + offset)

        w_raw = at("w_raw", [P, 2, 1280], F32, 0)
        w_hi = at("w_hi", [P, 2, 1280], F32R, 10240)
        w_lo = at("w_lo", [P, 2, 1280], F32R, 20480)
        h_hi = at("h_hi", [P, KT, T], F32R, 30720)
        h_lo = at("h_lo", [P, KT, T], F32R, 64512)
        C0 = 98304
        ident = at("ident", [P, P], F32, C0)
        mean1024 = at("mean1024", [P, P], F32, C0 + 512)
        mean256 = at("mean256", [P, P], F32, C0 + 1024)
        small = at("small", [P, 256], F32, C0 + 1536)
        ffn_w = at("ffn_w", [P, 2 * FT, 3], F32, C0 + 2560)
        ffn_state = at("ffn_state", [P, 2 * FT, NB * 2], F32, C0 + 3104)
        ffn_last = at("ffn_last", [P, 2 * FT, (NB + 1) * 2], F32, C0 + 5920)
        M0 = C0 + 9088
        X = at("X", [P, KT, T], F32, M0)
        Q0 = M0 + 33792
        g_cols = {n: small[:, 8 * i:8 * i + 8] for i, n in enumerate(("mix", "ffn", "ple", "final"))}
        eps_col = small[:, 32:33]
        sb_bias = small[:, 33:37]
        ln_c = small[:, 37:41]
        one_col = small[:, 110:111]
        conv_b_w = small[:, 41:47]
        conv_c_w = small[:, 47:47 + 2 * CW]

        q = at("q", [P, 2, T], F32, M0)
        k = at("k", [P, 2, T], F32, M0 + 8448)
        v = at("v", [P, 2, T], F32, M0 + 16896)
        vT = at("vT", [P, 9, W], F32, Q0)
        zb = at("zb", [P, 4, QC], F32, Q0 + 9216)
        le = at("le", [P, 2, QC], F32, Q0 + 17408)
        spl = at("softplus", [P, 2, QC], F32, Q0 + 21504)
        av = at("attend", [P, 3, QC], F32, Q0 + 25600)
        k_pages = at("k_pages", [P, 2, NB, 2 * PAGE], F32, Q0 + 31744)
        v_pages = at("v_pages", [P, NB, W], F32, Q0 + 48128)
        A0 = Q0 + 56320
        tri = at("tri", [P, P], F32, A0)
        comp = at("comp", [P, P], F32, A0 + 512)
        causal = at("causal", [P, 2, P], F32, A0 + 1024)
        own = at("own", [P, 2, P], F32, A0 + 2048)
        bcol = at("bcol", [P, P], F32, A0 + 3072)
        qbd = at("qbd", [P, 2, NB, 2, TS], F32, A0 + 3584)
        ptab = at("ptab", [1, NB * N_PAGES], I32, A0 + 4096)

        le_s = at("le_s", [P, 2, P], F32, Q0 + 19232)
        zb_s = at("zb_s", [P, 4, P], F32, Q0 + 20256)
        spl_s = at("softplus_s", [P, 2, P], F32, Q0 + 22304)
        av_s = at("attend_s", [P, 3, P], F32, Q0 + 23328)

        va = at("va", [P, 2, T], F32, M0 + 16896)
        side = at("side", [P, 2, T], F32, M0 + 8448)
        u = at("u", [P, 2, T], F32, M0 + 25344)
        vaT = at("vaT", [P, 9, W], F32, Q0 + 60672)
        lnv = at("lnv", [P, 2, W], F32, Q0 + 24864)
        wsp = at("wsp", [P, 4, P], F32, Q0 + 26912)
        bsp = at("bsp", [P, 2, P], F32, Q0 + 28960)
        bss = at("bss", [P, 2, NS], F32, Q0 + 29984)
        wss = at("wss", [NS, 4, NS], F32, Q0 + 30240)
        stat = at("stat", [P, 9, 8], F32, Q0 + 30752)
        pb = at("pb", [P, 2, LB], F32, Q0)
        pcv = at("pc", [P, 2, LC], F32, Q0 + 8608)
        bg = at("bg", [P, 2, T], F32, Q0 + 19232)
        acc = at("conv_sum", [P, LC - CW + 1], F32, Q0 + 27680)
        cv = at("cv", [P, 2, T], F32, Q0 + 8608)
        csq = at("csq", [P, 2, CH], F32, Q0 + 27680)
        cstd = at("cstd", [P, CH], F32, Q0 + 27680 + 2816)
        slots = at("slots", [P, 2, 2, 2, T], F32R, Q0 + 32896)
        slot_hi, slot_lo = slots[:, :, 0], slots[:, :, 1]
        gate = at("gate", [P, NCH, CH], F32, Q0 + 66688)
        gate_late = at("gate_late", [P, NCH, CH], F32, Q0 + 33792)
        x_again = at("x_again", [P, KT, T], F32, Q0)
        hid_hi = at("hid_hi", [P, 6, T], F32R, Q0)
        hid_lo = at("hid_lo", [P, 6, T], F32R, Q0 + 25344)
        up = at("up", [P, 2, LB], F32, Q0 + 50688)
        cu = at("cu", [P, 2, LB - 2], F32, Q0 + 59296)
        spare = [Q0 + 3 * 4224, Q0 + 5 * 4224, Q0 + 25344 + 3 * 4224, Q0 + 25344 + 5 * 4224]
        p_in = [at(f"p_in{t}", [P, T], F32, spare[t]) for t in range(2)]
        p_lo = [at(f"p_lo{t}", [P, T], F32R, spare[t]) for t in range(2)]
        p_hi = [at(f"p_hi{t}", [P, T], F32R, spare[2 + t]) for t in range(2)]
        norm_bufs = []
        for i, a in enumerate((Q0 + 38016, Q0 + 50688)):
            norm_bufs += 2 * [(at(f"sq{i}", [P, NCH, CH], F32, a),
                               at(f"ssum{i}", [P, NCH, CH], F32, a + 4224),
                               at(f"rstd{i}", [P, NCH, CH], F32, a + 8448),
                               at(f"nt{i}", [P, 4, CH], F32, a + 12672))]

        ps = ctx.enter_context(nc.psum_tensor("ps", [P, 8, 512], F32))

        w_in = [sem("w_in0"), sem("w_in1")]
        w_high = sem("w_high")
        w_split = sem("w_split")
        x_in = [sem(f"x_in{c}") for c in range(NCH)]
        consts_in = sem("consts_in")
        att_in = sem("att_in")
        mixc_in = sem("mixc_in")
        x2_in = sem("x2_in")
        a_full = sem("a_full")
        a_read = sem("a_read")
        d_full = sem("d_full")
        d_read = sem("d_read")
        n_sq = sem("n_sq")
        n_add = sem("n_add")
        n_sum = sem("n_sum")
        n_std = sem("n_std")
        n_t = sem("n_t")
        n_hi = sem("n_hi")
        n_lo, n_lo_dve = sem("n_lo"), sem("n_lo_dve")
        tr_full, tr_read = sem("tr_full"), sem("tr_read")
        z_full, z_read = sem("z_full"), sem("z_read")
        lch = sem("lch")
        l_ready, sp_ready = sem("l_ready"), sem("sp_ready")
        later_full, t_ready = sem("later_full"), sem("t_ready")
        a_ready, pv_done = sem("a_ready"), sem("pv_done")
        o_read = sem("o_read")
        qbd_ready = sem("qbd_ready")
        kp_in = [sem(f"kp_in{g}") for g in range(2)]
        vp_in = sem("vp_in")
        states_in = sem("states_in")
        dch = sem("dch")
        slot_ready = sem("slot_ready")
        out_kv = sem("out_kv")
        out_state = sem("out_state")
        out_va = sem("out_va")
        out_last = sem("out_last")
        out_y = sem("out_y")
        va_stat, va_std, va_done = sem("va_stat"), sem("va_std"), sem("va_done")
        mix_full, mix_read = sem("mix_full"), sem("mix_read")
        tables_masked = sem("tables_masked")
        pads_ready = sem("pads_ready")
        prod_done = sem("prod_done")
        c_conv, c_mean, c_cent, c_sq, c_var, c_std, c_norm, c_act = (sem(n) for n in (
            "c_conv", "c_mean", "c_cent", "c_sq", "c_var", "c_std", "c_norm", "c_act"))
        g_used = sem("g_used")
        m_high = sem("m_high")
        m_ready = sem("m_ready")
        up_used = sem("up_used")
        ga_act, prod_ready, hid_h, hid_ready = (sem(n) for n in (
            "ga_act", "prod_ready", "hid_h", "hid_ready"))
        p_land = sem("p_land")
        p_high, p_ready = sem("p_high"), sem("p_ready")

        phases = [("w_mix", 0, N_MIX, 1024), ("w_gate", 0, N_GATE, 1280), ("w_o", 0, KT, 1024)]
        f0 = 0
        for n, g in enumerate(GROUPS):
            phases += [("w_up", 2 * f0, 2 * UPS[n], 1024), ("w_down", KT * n, KT, 128 * g)]
            f0 += UPS[n]
        phases += [("w_ple", 0, KT, 1280)]
        first_tile = []
        n_tiles = 0
        for _, _, n, _ in phases:
            first_tile.append(n_tiles)
            n_tiles += n
        done_with = []
        na = nd = 0
        for name, _, n, _ in phases:
            if name in ("w_mix", "w_up"):
                done_with.append((a_full, na))
                na += n
            else:
                done_with.append((d_full, nd))
                nd += n
                na += n if name in ("w_gate", "w_ple") else 0

        def tokens(c):
            return slice(c * CH, (c + 1) * CH)

        def sample_cols(buf, pad):
            a = pad + TP
            return buf[:, a:a + NB * (pad + TS)].rearrange("p (b t) -> p b t", b=NB)[:, :, pad:]

        def sample_states(buf, pad):
            a = pad + TP
            return buf[:, a:a + NB * (pad + TS)].rearrange("p (b t) -> p b t", b=NB)[:, :, :pad]

        def last_cols(buf, pad):
            return buf[:, TP - TS:].rearrange("p (b t) -> p b t", b=NB + 1)[:, :, TS:]

        def as_samples(ap):
            return ap.rearrange("p (b t) -> p b t", b=NB)


        def normed_tiles(ph):
            return sum(n for name, _, n, _ in phases[:ph] if name in ("w_mix", "w_gate", "w_up"))

        def d_tiles(ph):
            return sum(n for name, _, n, _ in phases[:ph] if name not in ("w_mix", "w_up"))

        UP = [3 + 2 * g for g in range(len(GROUPS))]
        DOWN = [4 + 2 * g for g in range(len(GROUPS))]
        PLE = len(phases) - 1

        DVE_LOWS = (3, 7)

        def lows_done(i):
            by_dve = sum(1 for t in DVE_LOWS if t <= i % KT) + len(DVE_LOWS) * (i // KT)
            return (n_lo_dve, by_dve) if i % KT in DVE_LOWS else (n_lo, i + 1 - by_dve)

        def adds(n, i):
            return i + (27 * n + 4)

        def hidden_slots(g):
            return [AHEAD[g]] + list(range(GROUPS[g] - 1)) if g else list(range(GROUPS[0]))

        def offset(i):
            _, qc, kb = units[i]
            return max(0, kb * P - qc * QC)

        def width(i):
            return slice(offset(i), QC) if i < NU else slice(0, P)

        def keys(i):
            return NS if i == NU else P

        def is_first(i):
            return units[i][2] == (units[i][1] + 1) * QC // P - 1 if i < NU else i == NU

        def is_last(i):
            return units[i][2] == 0 if i < NU else i == STEPS - 1

        def on_diagonal(i):
            return units[i][2] * P >= units[i][1] * QC if i < NU else i == NU

        SLOTS = N_PAGES + 3

        def bufs(i):
            if i < NU:
                return zb[:, i % 4], le[:, i % 2], spl[:, i % 2], av[:, i % 3]
            return zb_s[:, i % 4], le_s[:, i % 2], spl_s[:, i % 2], av_s[:, i % 3]

        def z_bank(i):
            return 5 + i % 2 if i < NU else 5

        def chains_before(i):
            return sum(1 for j in range(min(i, STEPS)) if is_last(j))

        def pages(engine, g, cache, ring, landed):
            page = N_PAGES - 1 - g
            for b in range(NB):
                phys = engine.value_load(ptab[0:1, b * N_PAGES + page:b * N_PAGES + page + 1],
                                         min_val=0, max_val=N_PHYS - 1)
                src = d[cache][bass.ds(phys, 1)].rearrange("a p n -> p (a n)")
                engine.dma_start(ring[:, b, :], src).then_inc(landed, 16)

        block = ctx.enter_context(nc.Block())

        @block.sync
        def _(sp):
            def weights(ph, p0=0, p1=None):
                name, t0, n, cols = phases[ph]
                b = first_tile[ph]
                p1 = n // 2 if p1 is None else p1

                def one(p, j):
                    src = d[name][bass.ds(p * 2 + (t0 + j), 1), :, 0:cols]
                    sp.dma_start(w_raw[:, j, 0:cols], src.rearrange("a p n -> p (a n)")
                                 ).then_inc(w_in[j], 16)

                with sp.Fori(p0, p1) as p:
                    for j in range(2):
                        sp.wait_ge(w_split, p * 2 + (b + j - 1))
                        one(p, j)

            sp.dma_start(X[:, :, tokens(0)], d["x"][0]).then_inc(x_in[0], 16)
            for name, dst in (("small", small), ("mean1024", mean1024), ("mean256", mean256),
                              ("ident", ident), ("ffn_w", ffn_w), ("ffn_state", ffn_state)):
                sp.dma_start(dst[:], d[name]).then_inc(consts_in, 16)
            for j in range(2):
                sp.dma_start(X[:, :, tokens(1 + j)], d["x"][1 + j]).then_inc(x_in[1 + j], 16)
                sp.dma_start(w_raw[:, j, 0:1024], d["w_mix"][j]).then_inc(w_in[j], 16)
            for name, dst in (("tri", tri), ("comp", comp), ("causal", causal), ("own", own),
                              ("bcol", bcol), ("ptab", ptab)):
                sp.dma_start(dst[:], d[name]).then_inc(att_in, 16)
            weights(0, 1, 4)
            sp.wait_ge(att_in, 16 * 6)

            def keys_of(g):
                pages(sp, g, "cache_kT", k_pages[:, g % 2], kp_in[g % 2])

            keys_of(0)
            keys_of(1)
            pages(sp, 0, "cache_v", v_pages, vp_in)
            sp.wait_ge(o_read, chains_before(NU))
            for name, dst in (("lnv", lnv), ("wsp", wsp), ("bsp", bsp), ("bss", bss), ("wss", wss)):
                sp.dma_start(dst[:], d[name]).then_inc(mixc_in, 16)
            for n in range(8, N_MIX):
                sp.wait_ge(w_split, n - 1)
                sp.dma_start(w_raw[:, n % 2, 0:1024], d["w_mix"][n]).then_inc(w_in[n % 2], 16)
                s = n - 9
                if 2 <= s + 1 < N_PAGES:
                    sp.wait_ge(z_full, NU + s + 1)
                    keys_of(s + 1)
                if s == 2:
                    sp.wait_ge(pv_done, NU + 1)
                    for t in range(2):
                        sp.dma_start(sample_states(pb[:, t, :], 2), d["state_b"][t]
                                     ).then_inc(states_in, 16)
                        sp.dma_start(sample_states(pcv[:, t, :], CW - 1), d["state_c"][t]
                                     ).then_inc(states_in, 16)
            weights(1, 0, 13)
            sp.wait_ge(slot_ready, 4)
            sp.wait_ge(out_state, 16 * 4)
            sp.wait_ge(g_used, 3 * 24)
            for p in range(13, 16):
                weights(1, p, p + 1)
                for m in range(3 * (p - 13), min(KT, 3 * (p - 12))):
                    sp.dma_start(x_again[:, m, :].rearrange("p (c n) -> p c n", c=NCH),
                                 d["x"][:, :, m, :].rearrange("c p n -> p c n")).then_inc(x2_in, 16)
            for ph in range(2, PLE):
                weights(ph)
                if ph == UP[-1]:
                    sp.wait_ge(d_read, 3 * d_tiles(DOWN[-1]))
                    for t in range(2):
                        sp.dma_start(p_in[t][:], d["p"][:, t, :]).then_inc(p_land, 16)
            weights(PLE)
            for c in range(NCH):
                for h in range(2):
                    sp.wait_ge(n_t, 24 * 3 + 8 * c + 4 * h + 4)
                    t = slice(4 * h, 4 * h + 4)
                    sp.dma_start(d["y"][t, :, tokens(c)].rearrange("t p n -> p t n"),
                                 X[:, t, tokens(c)]).then_inc(out_y, 16)
            sp.wait_ge(out_y, 16 * 6)

        @block.gpsimd
        def _(pool):
            def lows(n, c):
                nt = norm_bufs[n][3]
                for t in range(KT):
                    if t in DVE_LOWS:
                        continue
                    i = 8 * (NCH * n + c) + t
                    pool.wait_ge(n_hi, i + 1)
                    pool.tensor_tensor(h_lo[:, t, tokens(c)], nt[:, t % 4, :],
                                       h_hi[:, t, tokens(c)], ALU.subtract).then_inc(n_lo, 1)

            def split(ph, p0=0, p1=None, norm=None):
                _, _, n, cols = phases[ph]
                b = first_tile[ph]
                p1 = n // 2 if p1 is None else p1

                def one(p, j):
                    pool.wait_ge(w_in[j], p * 16 + 16 * (b // 2 + 1))
                    raw, hi, lo = w_raw[:, j, 0:cols], w_hi[:, j, 0:cols], w_lo[:, j, 0:cols]
                    pool.tensor_tensor(hi, raw, one_col.to_broadcast([P, cols]), ALU.mult
                                       ).then_inc(w_high, 1)
                    pool.wait_ge(w_high, p * 2 + (b + j + 1))
                    pool.tensor_tensor(lo, raw, hi, ALU.subtract).then_inc(w_split, 1)

                if p0 == 0:
                    for j in range(2):
                        if ph > 0:
                            s, first = done_with[ph - 1]
                            pool.wait_ge(s, 3 * (first + phases[ph - 1][2] - 1 + j))
                        one(0, j)
                        if norm is not None:
                            for c in ((0, 1), (2,))[j]:
                                lows(norm, c)
                    p0 = 1
                s, first = done_with[ph]
                with pool.Fori(p0, p1) as p:
                    for j in range(2):
                        pool.wait_ge(s, p * 6 + 3 * (first + j - 1))
                        one(p, j)

            pool.wait_ge(consts_in, 16 * 6)
            split(0, 0, 4, norm=0)
            pool.wait_ge(mixc_in, 16 * 5)
            pool.affine_select(out=wsp[:], in_=wsp[:], compare_op=ALU.is_ge, fill=0.0, base=0,
                               pattern=[[0, 4], [1, P]], channel_multiplier=-1
                               ).then_inc(tables_masked, 1)
            pool.affine_select(out=wss[:], in_=wss[:], compare_op=ALU.is_ge, fill=0.0, base=0,
                               pattern=[[0, 4], [1, NS]], channel_multiplier=-1
                               ).then_inc(tables_masked, 1)
            split(0, 4)
            for ph in range(1, len(phases)):
                split(ph, norm={UP[0]: 1, PLE: 2}.get(ph))

        @block.tensor
        def _(pe):
            def product(j, blocks, rhs_hi, rhs_lo, out, full):
                last = 3 * len(blocks) - 1
                m = 0
                for i, b in enumerate(blocks):
                    wh = w_hi[:, j, b * P:(b + 1) * P]
                    wl = w_lo[:, j, b * P:(b + 1) * P]
                    for w_, r_ in ((wh, rhs_hi(i)), (wh, rhs_lo(i)), (wl, rhs_hi(i))):
                        mm = pe.matmul(out, w_, r_, start=(m == 0), stop=(m == last))
                        m += 1
                mm.then_inc(full, 1)

            def norm_sum(n, c):
                m = NCH * n + c
                pe.wait_ge(n_add, adds(n, 8 * c + 7 if n == 0 else 21 + c))
                if m >= 2:
                    pe.wait_ge(n_std, m - 1)
                pe.matmul(ps[:, 6 + m % 2, 0:CH], mean1024[:], norm_bufs[n][1][:, c, :],
                          start=True, stop=True).then_inc(n_sum, 1)

            def a_tile(p, j, b, a, norm=None, after=None):
                for c in range(NCH):
                    if norm == 0 and c < 2:
                        for c1 in ((0, 1), (2,))[c]:
                            norm_sum(0, c1)
                    if c == 0:
                        pe.wait_ge(w_split, p * 2 + (b + j + 1))
                    if norm is not None:
                        for t in (6, 7):
                            pe.wait_ge(*lows_done(KT * (NCH * norm + c) + t))
                    if norm != 0:
                        pe.wait_ge(a_read, a * 3 + (c - 2))
                    product(j, range(8), lambda i: h_hi[:, i, tokens(c)],
                            lambda i: h_lo[:, i, tokens(c)], ps[:, c, 0:CH], a_full)
                    if after is not None:
                        after(c)

            def d_tile(j, dn, blocks, rhs_hi, rhs_lo, norm=None, first=None):
                for c in range(NCH):
                    if not (isinstance(dn, int) and dn == 0):
                        pe.wait_ge(d_read, dn * 3 + (c - 2))
                    if first is not None:
                        first(c)
                    product(j, blocks, lambda i: rhs_hi(i, c), lambda i: rhs_lo(i, c),
                            ps[:, 3 + c, 0:CH], d_full)
                    if norm is not None and c >= 1:
                        norm_sum(norm, c - 1)
                if norm is not None:
                    norm_sum(norm, NCH - 1)

            def transpose(src, n, bank):
                blk = n % 9
                w_ = P if blk < 8 else NS
                if n >= 2:
                    pe.wait_ge(tr_read, n - 1)
                for t in range(2):
                    mm = pe.transpose(ps[0:w_, bank, t * P:(t + 1) * P],
                                      src[:, t, blk * P:blk * P + w_], ident[:])
                mm.then_inc(tr_full, 1)

            pe.wait_ge(consts_in, 16 * 6)
            for n in range(6):
                a_tile(n // 2, n % 2, 0, n, norm=0 if n == 0 else None)
            pe.wait_ge(a_read, 18)
            for n in range(9):
                transpose(v, n, 6 + n % 2)

            pe.wait_ge(att_in, 16 * 6)
            pe.wait_ge(tr_read, 9)

            def scores(i):
                if i >= NU:
                    pe.wait_ge(z_read, i)
                elif i >= 2:
                    pe.wait_ge(z_read, i - 1)
                bank = z_bank(i)
                if i < NU:
                    h, qc, kb = units[i]
                    r = slice(HD * (h % 2), HD * (h % 2) + HD)
                    mm = pe.matmul(ps[:, bank, width(i)], k[r, h // 2, kb * P:(kb + 1) * P],
                                   q[r, h // 2, qc * QC + offset(i):(qc + 1) * QC],
                                   start=True, stop=True)
                elif i == NU:
                    pe.wait_ge(qbd_ready, 1)
                    for hp in range(2):
                        mm = pe.matmul(ps[0:NS, bank, hp * 64:(hp + 1) * 64], k[:, hp, TP:T],
                                       qbd[:, hp].rearrange("p b h t -> p (b h t)"),
                                       start=True, stop=True)
                else:
                    g = i - NU - 1
                    pe.wait_ge(kp_in[g % 2], 16 * NB * (g // 2 + 1))
                    for hp in range(2):
                        for b in range(NB):
                            col = hp * 64 + b * 8
                            mm = pe.matmul(ps[:, bank, col:col + 8],
                                           k_pages[:, g % 2, b, hp * PAGE:(hp + 1) * PAGE],
                                           qbd[:, hp, b].rearrange("p h t -> p (h t)"),
                                           start=True, stop=True)
                mm.then_inc(z_full, 1)

            def chain_bank(i):
                return 3 + units[i][0] % 2 if i < NU else 3

            def later(i):
                pe.wait_ge(sp_ready, i + 1)
                n = keys(i)
                pe.matmul(ps[:, chain_bank(i), width(i)], tri[0:n, :], bufs(i)[2][0:n, width(i)],
                          start=is_first(i), stop=is_last(i), skip_group_check=True
                          ).then_inc(later_full, 1)

            def rest(i):
                pe.wait_ge(t_ready, i + 1)
                if not is_last(i):
                    n = keys(i)
                    pe.matmul(ps[:, chain_bank(i), width(i)], comp[0:n, :],
                              bufs(i)[2][0:n, width(i)], start=False, stop=False,
                              skip_group_check=True)

            def values(i):
                pe.wait_ge(a_ready, i + 1)
                if is_first(i) and chains_before(i):
                    pe.wait_ge(o_read, chains_before(i))
                if i < NU:
                    h, qc, kb = units[i]
                    r = HD * (h % 2)
                    mm = pe.matmul(ps[r:r + HD, 7, width(i)], vT[:, kb, h * HD:(h + 1) * HD],
                                   bufs(i)[3][:, width(i)], start=is_first(i), stop=is_last(i),
                                   skip_group_check=True)
                elif i == NU:
                    for hp in range(2):
                        mm = pe.matmul(ps[:, 7, hp * 64:(hp + 1) * 64],
                                       vT[0:NS, 8, hp * P:(hp + 1) * P],
                                       bufs(i)[3][0:NS, hp * 64:(hp + 1) * 64],
                                       start=(hp == 0), stop=False, skip_group_check=True)
                else:
                    g = i - NU - 1
                    pe.wait_ge(vp_in, 16 * NB * (g + 1))
                    for hp in range(2):
                        for b in range(NB):
                            col = hp * 64 + b * 8
                            mm = pe.matmul(ps[:, 7, col:col + 8],
                                           v_pages[:, b, hp * P:(hp + 1) * P],
                                           bufs(i)[3][:, col:col + 8], start=False,
                                           stop=is_last(i), skip_group_check=True)
                mm.then_inc(pv_done, 1)

            scores(0)
            scores(1)
            for i in range(NU + 2):
                if i + 2 < NU:
                    scores(i + 2)
                if 1 <= i <= NU:
                    rest(i - 1)
                if i < NU:
                    later(i)
                if i >= 2:
                    values(i - 2)

            def turn(s):
                if s <= N_PAGES:
                    scores(NU + s)
                if 2 <= s:
                    rest(NU + s - 2)
                if 1 <= s <= N_PAGES + 1:
                    later(NU + s - 1)
                if 2 <= s:
                    values(NU + s - 2)

            def spatial(m):
                if m == 0:
                    pe.wait_ge(va_done, 9)
                    pe.wait_ge(tables_masked, 2)
                if m >= 2:
                    pe.wait_ge(mix_read, m - 1)
                if m < 4:
                    t, half = m // 2, m % 2
                    for c4 in range(4):
                        for g in range(2):
                            f = (2 * t + g) * 64
                            mm = pe.matmul(ps[64 * g:64 * g + 64, 4 + 2 * half,
                                              c4 * P:(c4 + 1) * P],
                                           vaT[:, 4 * half + c4, f:f + 64], wsp[:, 2 * t + g, :],
                                           start=True, stop=True)
                else:
                    for t in range(2):
                        for g in range(2):
                            f = (2 * t + g) * 64
                            mm = pe.matmul(ps[64 * g:64 * g + 64, 4, t * NS:(t + 1) * NS],
                                           vaT[0:NS, 8, f:f + 64], wss[:, 2 * t + g, :],
                                           start=True, stop=True)
                mm.then_inc(mix_full, 1)

            for n in range(6, 18):
                def between(c):
                    x = 3 * (n - 6) + c
                    if c == 0 and n - 6 < SLOTS:
                        turn(n - 6)
                    if 6 <= x < 15:
                        transpose(va, x + 3, 4 + 2 * (x % 2))
                    if 21 <= x < 26:
                        spatial(x - 21)

                a_tile(n // 2, n % 2, 0, n, after=between)
            for n in range(18, 20):
                a_tile(n // 2, n % 2, 0, n)
            pe.wait_ge(o_read, chains_before(STEPS))
            pe.wait_ge(z_read, STEPS)

            def norm_of_c(m):
                if m >= 2 * NCH:
                    return
                c = m // 2
                if m % 2 == 0:
                    pe.wait_ge(c_conv, 2)
                    for t in range(2):
                        mm = pe.matmul(ps[:, 6, 0:CH], mean256[:], cv[:, t, tokens(c)],
                                       start=(t == 0), stop=(t == 1))
                    mm.then_inc(c_mean, 1)
                else:
                    pe.wait_ge(c_sq, c + 1)
                    for t in range(2):
                        mm = pe.matmul(ps[:, 7, 0:CH], mean256[:], csq[:, t, :],
                                       start=(t == 0), stop=(t == 1))
                    mm.then_inc(c_var, 1)

            for br in range(4):
                s = br % 2
                pe.wait_ge(slot_ready, br + 1)

                def gate_and_branch(p, after=None):
                    for j in range(2):
                        a_tile(p, j, first_tile[1] + 8 * br, p * 2 + (N_MIX + 8 * br + j))
                        d_tile(j, p * 2 + (8 * br + j), (8, 9),
                               lambda i, c: slot_hi[:, s, i, tokens(c)],
                               lambda i, c: slot_lo[:, s, i, tokens(c)])
                        if after is not None:
                            after(p * 2 + j)

                if br == 2:
                    for p in range(KT // 2):
                        gate_and_branch(p, norm_of_c)
                    continue
                if br == 0:
                    pe.wait_ge(mix_read, 5)
                    gate_and_branch(0)
                with pe.Fori(1 if br == 0 else 0, KT // 2) as p:
                    gate_and_branch(p)

            def o_tile(p, j, norm=None, first=None):
                pe.wait_ge(w_split, p * 2 + (first_tile[2] + j + 1))
                d_tile(j, p * 2 + (d_tiles(2) + j), range(8),
                       lambda i, c: h_hi[:, i, tokens(c)], lambda i, c: h_lo[:, i, tokens(c)],
                       norm, first)

            o_tile(0, 0, first=lambda c: pe.wait_ge(m_ready, c + 1))
            o_tile(0, 1)
            with pe.Fori(1, KT // 2 - 1) as p:
                o_tile(p, 0)
                o_tile(p, 1)
            o_tile(KT // 2 - 1, 0)
            o_tile(KT // 2 - 1, 1, norm=1)

            for g, size in enumerate(GROUPS):
                if g == 0:
                    a_tile(0, 0, first_tile[UP[0]], normed_tiles(UP[0]), norm=1)
                    a_tile(0, 1, first_tile[UP[0]], normed_tiles(UP[0]) + 1)
                with pe.Fori(1 if g == 0 else 0, UPS[g]) as f:
                    for j in range(2):
                        a_tile(f, j, first_tile[UP[g]], f * 2 + (normed_tiles(UP[g]) + j))
                last = g == len(GROUPS) - 1
                where = hidden_slots(g)

                def down_tile(p, j, norm=None):
                    pe.wait_ge(w_split, p * 2 + (first_tile[DOWN[g]] + j + 1))
                    d_tile(j, p * 2 + (d_tiles(DOWN[g]) + j), range(size),
                           lambda i, c: hid_hi[:, where[i], tokens(c)],
                           lambda i, c: hid_lo[:, where[i], tokens(c)], norm)

                if last:
                    dn = d_tiles(DOWN[g])
                    pe.wait_ge(w_split, first_tile[DOWN[g]] + 1)
                    pe.wait_ge(hid_ready, FT - 1)
                    for half in range(2):
                        if half:
                            pe.wait_ge(hid_ready, FT)
                        for c in range(NCH):
                            if not half:
                                pe.wait_ge(d_read, dn * 3 + (c - 2))
                            for i in (range(size - 1, size) if half else range(size - 1)):
                                wh, wl = (w_[:, 0, i * P:(i + 1) * P] for w_ in (w_hi, w_lo))
                                hh, hl = (b[:, where[i], tokens(c)] for b in (hid_hi, hid_lo))
                                for n, (w_, r_) in enumerate(((wh, hh), (wh, hl), (wl, hh))):
                                    mm = pe.matmul(ps[:, 3 + c, 0:CH], w_, r_,
                                                   start=(i == 0 and n == 0),
                                                   stop=(half == 1 and n == 2))
                            if half:
                                mm.then_inc(d_full, 1)
                else:
                    pe.wait_ge(hid_ready, sum(GROUPS[:g + 1]))
                    down_tile(0, 0)
                down_tile(0, 1)
                with pe.Fori(1, KT // 2 - 1) as p:
                    down_tile(p, 0)
                    down_tile(p, 1)
                down_tile(KT // 2 - 1, 0)
                down_tile(KT // 2 - 1, 1, norm=2 if last else None)

            def embedding_tile(p, j, norm=None):
                a_tile(p, j, first_tile[PLE], p * 2 + (normed_tiles(PLE) + j), norm)
                if norm is not None:
                    pe.wait_ge(p_ready, 2)
                d_tile(j, p * 2 + (d_tiles(PLE) + j), (8, 9),
                       lambda i, c: p_hi[i][:, tokens(c)], lambda i, c: p_lo[i][:, tokens(c)])

            embedding_tile(0, 0, norm=2)
            embedding_tile(0, 1)
            with pe.Fori(1, KT // 2) as p:
                embedding_tile(p, 0)
                embedding_tile(p, 1)
            for c in range(NCH):
                norm_sum(3, c)

        @block.scalar
        def _(act):
            def square(n, i, c, x):
                act.wait_ge(n_add, i + (27 * n + 1))
                act.activation(norm_bufs[n][0][:, c, :], x, ACT.Square).then_inc(n_sq, 1)

            def squares_of_tile(n, p, j, done, count, chunks=range(NCH)):
                for c in chunks:
                    act.wait_ge(done, p * 6 + (count + 3 * j + c + 1))
                    square(n, p * 6 + (3 * j + c), c,
                           X[:, bass.ds(p * 2 + j, 1), tokens(c)].rearrange("p a n -> p (a n)"))

            def root(n, c):
                m = NCH * n + c
                act.wait_ge(n_sum, m + 1)
                act.activation(norm_bufs[n][2][:, c, :], ps[:, 6 + m % 2, 0:CH], ACT.Sqrt,
                               bias=eps_col).then_inc(n_std, 1)

            def highs(n, c):
                for t in range(KT):
                    act.wait_ge(n_t, 8 * (NCH * n + c) + t + 1)
                    act.activation(h_hi[:, t, tokens(c)], norm_bufs[n][3][:, t % 4, :], ACT.Copy
                                   ).then_inc(n_hi, 1)

            def squares_and_norm(n, ph):
                count = 3 * d_tiles(ph)
                with act.Fori(0, KT // 2 - 1) as p:
                    for j in range(2):
                        squares_of_tile(n, p, j, d_read, count)
                p = KT // 2 - 1
                act.preload_act_table_set("sqrt_and_others")
                squares_of_tile(n, p, 0, d_read, count)
                squares_of_tile(n, p, 1, d_read, count, (0, 1))
                root(n, 0)
                highs(n, 0)
                squares_of_tile(n, p, 1, d_read, count, (2,))
                for c in (1, 2):
                    root(n, c)
                    highs(n, c)

            def evacuate(a, dst, func=ACT.Copy, after_first=lambda: None):
                for c in range(NCH):
                    act.wait_ge(a_full, a * 3 + (c + 1))
                    act.activation(dst[:, tokens(c)], ps[:, c, 0:CH], func).then_inc(a_read, 1)
                    if c == 0:
                        after_first()

            def evacuate_padded(a, dst, pad, after_first=lambda: None):
                for c in range(NCH):
                    act.wait_ge(a_full, a * 3 + (c + 1))
                    if c < NCH - 1:
                        act.activation(dst[:, pad + c * CH:pad + (c + 1) * CH], ps[:, c, 0:CH],
                                       ACT.Copy).then_inc(a_read, 1)
                        if c == 0:
                            after_first()
                    else:
                        act.activation(dst[:, pad + c * CH:pad + TP], ps[:, c, 0:PC], ACT.Copy)
                        act.activation(sample_cols(dst, pad), as_samples(ps[:, c, PC:CH]),
                                       ACT.Copy).then_inc(a_read, 1)

            act.wait_ge(consts_in, 16 * 6)
            def squares_of_chunk(c):
                act.wait_ge(x_in[c], 16)
                for t in range(KT):
                    i = KT * c + t
                    square(0, i, i % 3, X[:, t, tokens(c)])

            act.preload_act_table_set("sqrt_and_others")
            squares_of_chunk(0)
            root(0, 0)
            highs(0, 0)
            squares_of_chunk(1)
            squares_of_chunk(2)
            for c in (1, 2):
                root(0, c)
                highs(0, c)
            for n, dst in enumerate((q, q, k, k, v, v)):
                evacuate(n, dst[:, n % 2, :])
            act.wait_ge(a_read, 18)
            act.dma_start(d["k_out"], k[:]).then_inc(out_kv, 16)
            act.dma_start(d["v_out"], v[:]).then_inc(out_kv, 16)

            def softplus_part(i):
                w, n = width(i), keys(i)
                z, out = bufs(i)[0][0:n, w], bufs(i)[1][0:n, w]
                act.wait_ge(z_read, i + 1)
                if i >= 2:
                    act.wait_ge(sp_ready, i - 1)
                act.activation(out, z, ACT.Abs).then_inc(lch, 1)
                act.wait_ge(lch, 2 * i + 1)
                act.activation(out, out, ACT.Exp, scale=-1.0).then_inc(lch, 1)
                act.wait_ge(lch, 2 * i + 2)
                act.activation(out, out, ACT.Ln, bias=one_col[0:n]).then_inc(l_ready, 1)

            def weights_of(i):
                w, n = width(i), keys(i)
                act.wait_ge(t_ready, i + 1)
                if i >= 3:
                    act.wait_ge(pv_done, i - 2)
                act.activation(bufs(i)[3][0:n, w], bufs(i)[0][0:n, w], ACT.Exp).then_inc(a_ready, 1)

            act.preload_act_table_set("natural_log_exp_and_others")
            softplus_part(0)
            for i in range(NU + 1):
                if i + 1 < NU:
                    softplus_part(i + 1)
                if i >= 1:
                    weights_of(i - 1)

            def turn(s):
                if s < SLOTS:
                    act.preload_act_table_set("natural_log_exp_and_others")
                    if s <= N_PAGES:
                        softplus_part(NU + s)
                    if 1 <= s <= N_PAGES + 1:
                        weights_of(NU + s - 1)
                    if 1 <= s - 2 < N_PAGES:
                        act.wait_ge(pv_done, NU + s - 1)
                        pages(act, s - 2, "cache_v", v_pages, vp_in)

            act.wait_ge(out_kv, 16 * 2)
            for n in range(6, 8):
                evacuate(n, va[:, n % 2, :], ACT.Gelu_apprx_tanh, lambda: turn(n - 6))
            for n in range(8, 10):
                evacuate(n, u[:, n % 2, :], ACT.Gelu_apprx_tanh, lambda: turn(n - 6))
            act.wait_ge(pads_ready, 4)
            for t in range(2):
                evacuate_padded(10 + 2 * t, pb[:, t, :], 2, lambda: turn(4 + 2 * t))
                evacuate(11 + 2 * t, side[:, t, :], ACT.Copy, lambda: turn(5 + 2 * t))
                if t == 0:
                    act.wait_ge(va_stat, 9)
                    act.activation(stat[:, 0:8, 4:5], stat[:, 0:8, 7:8], ACT.Sqrt, bias=eps_col)
                    act.activation(stat[0:NS, 8:9, 4:5], stat[0:NS, 8:9, 7:8], ACT.Sqrt,
                                   bias=eps_col[0:NS]).then_inc(va_std, 1)
            for t in range(2):
                evacuate_padded(14 + 2 * t, pcv[:, t, :], CW - 1, lambda: turn(8 + 2 * t))
                act.wait_ge(prod_done, t + 1)
                evacuate(15 + 2 * t, side[:, t, :], ACT.Sigmoid, lambda: turn(9 + 2 * t))
            act.wait_ge(va_done, 9)
            act.dma_start(d["va_out"], vaT[0:NS, 8, :]).then_inc(out_va, 16)
            for t in range(2):
                act.wait_ge(prod_done, t + 1)
                act.dma_start(d["b_last"][t], last_cols(pb[:, t, :], 2)).then_inc(out_state, 16)
            for t in range(2):
                act.wait_ge(prod_done, t + 3)
                act.dma_start(d["c_last"][t], last_cols(pcv[:, t, :], CW - 1)
                              ).then_inc(out_state, 16)
            act.wait_ge(slot_ready, 1)
            for n in range(18, 20):
                evacuate(n, bg[:, n % 2, :])

            def gates(p, j, a, used, gate=gate):
                for c in range(NCH):
                    act.wait_ge(a_full, p * 6 + ((a + j) * 3 + c + 1))
                    if not (isinstance(p, int) and p == 0 and used + j == 0):
                        act.wait_ge(g_used, p * 6 + ((used + j) * 3 + c - 2))
                    act.activation(gate[:, c, :], ps[:, c, 0:CH], ACT.Sigmoid).then_inc(a_read, 1)

            act.wait_ge(out_va, 16)
            for br in range(4):
                if br == 2:
                    for m in range(KT):
                        gates(m // 2, m % 2, N_MIX + 16, 16)
                        c = m // 2
                        if c < NCH and m % 2 == 0:
                            act.wait_ge(c_cent, c + 1)
                            act.activation(csq[:], cv[:, :, tokens(c)], ACT.Square
                                           ).then_inc(c_sq, 1)
                        elif c < NCH:
                            act.wait_ge(c_var, c + 1)
                            if c:
                                act.wait_ge(c_norm, c)
                            act.activation(cstd[:], ps[:, 7, 0:CH], ACT.Sqrt, bias=eps_col
                                           ).then_inc(c_std, 1)
                        elif m == 2 * NCH:
                            act.wait_ge(c_norm, NCH)
                            for t in range(2):
                                act.activation(cv[:, t, :], cv[:, t, :], ACT.Silu,
                                               scale=ln_c[:, t:t + 1], bias=ln_c[:, 2 + t:3 + t]
                                               ).then_inc(c_act, 1)
                    continue
                if br == 0:
                    for j in range(2):
                        gates(0, j, N_MIX, 0)
                with act.Fori(1 if br == 0 else 0, KT // 2) as p:
                    for j in range(2):
                        gates(p, j, N_MIX + 8 * br, 8 * br, gate_late if br == 3 else gate)
            for c in range(NCH):
                act.wait_ge(g_used, 3 * (N_GATE - 1) + c + 1)
                act.activation(h_hi[:, :, tokens(c)], X[:, :, tokens(c)], ACT.Copy
                               ).then_inc(m_high, 1)
            squares_and_norm(1, 2)

            def up_tile(f, j, a, tile):
                buf = up[:, j, :]
                act.wait_ge(up_used, f * 2 + (tile + j + 1))
                act.activation(sample_states(buf, 2), as_samples(
                    ffn_state[:, bass.ds(f * 2 + (tile + j), 1), :].rearrange("p a n -> p (a n)")),
                    ACT.Copy)
                evacuate_padded(f * 2 + (a + j), buf, 2)

            def hidden(f, g, tile, slot):
                up_tile(f, 0, normed_tiles(UP[g]), 2 * tile)
                up_tile(f, 1, normed_tiles(UP[g]), 2 * tile)
                act.wait_ge(up_used, f * 2 + (2 * tile + 3))
                act.activation(cu[:, 0, :], cu[:, 0, :], ACT.Silu).then_inc(ga_act, 1)
                act.wait_ge(prod_ready, f + (tile + 1))
                act.activation(hid_hi[:, bass.ds(slot, 1), 0:TP].rearrange("p a n -> p (a n)"),
                               cu[:, 1, 0:TP], ACT.Copy)
                act.activation(as_samples(hid_hi[:, bass.ds(slot, 1), TP:T]
                                          .rearrange("p a n -> p (a n)")),
                               cu[:, 1, TP:].rearrange("p (b t) -> p b t", b=NB)[:, :, 2:],
                               ACT.Copy).then_inc(hid_h, 1)

            f0 = 0
            for g in range(len(GROUPS)):
                own_tiles = sum(GROUPS[:g + 1]) - f0
                with act.Fori(0, own_tiles) as f:
                    hidden(f, g, f0, f)
                if g + 1 < len(GROUPS):
                    hidden(own_tiles, g, f0, AHEAD[g + 1])
                f0 += UPS[g]
            act.wait_ge(up_used, 2 * FT + 2)
            act.dma_start(d["ffn_last"], ffn_last[:]).then_inc(out_last, 16)
            act.wait_ge(p_land, 16 * 2)
            for t in range(2):
                act.activation(p_hi[t][:], p_in[t][:], ACT.Copy).then_inc(p_high, 1)
            squares_and_norm(2, DOWN[-1])

            with act.Fori(0, KT // 2) as p:
                for j in range(2):
                    gates(p, j, normed_tiles(PLE), N_GATE, gate_late)
                    squares_of_tile(3, p, j, g_used, 3 * N_GATE)
            act.preload_act_table_set("sqrt_and_others")
            for c in range(NCH):
                root(3, c)
            act.wait_ge(out_last, 16)

        @block.vector
        def _(dve):
            chain = [0]

            def link(ins):
                ins.then_inc(dch, 1)
                chain[0] = chain[0] + 1
                dve.wait_ge(dch, chain[0])

            class Loop:

                def __init__(self, start, end, per):
                    self.start, self.end, self.per = start, end, per

                def __enter__(self):
                    self.before = chain[0]
                    self.loop = dve.Fori(self.start, self.end)
                    i = self.loop.__enter__()
                    chain[0] = (i - self.start) * self.per + self.before if self.start else \
                        i * self.per + self.before
                    return i

                def __exit__(self, *a):
                    self.loop.__exit__(*a)
                    chain[0] = self.before + (self.end - self.start) * self.per

            def clear_sums(n):
                dve.memset(norm_bufs[n][1][:], 0.0).then_inc(n_add, 3)

            def add_square(n, i, c, s):
                dve.wait_ge(n_sq, i + (24 * n + 1))
                dve.wait_ge(n_add, i + (27 * n + (3 if n == 0 else 1)))
                total = norm_bufs[n][1][:, c, :]
                dve.tensor_tensor(total, total, norm_bufs[n][0][:, s, :], ALU.add
                                  ).then_inc(n_add, 1)

            def scale(n, c, gains, last=False):
                m = NCH * n + c
                rstd = norm_bufs[n][2][:, c, :]
                dve.wait_ge(n_std, m + 1)
                link(dve.reciprocal(rstd, rstd))

                def low(t):
                    dve.wait_ge(n_hi, KT * m + t + 1)
                    dve.tensor_tensor(h_lo[:, t, tokens(c)], norm_bufs[n][3][:, t % 4, :],
                                      h_hi[:, t, tokens(c)], ALU.subtract).then_inc(n_lo_dve, 1)

                for t in range(KT):
                    i = KT * m + t
                    if not last and t - 2 in DVE_LOWS:
                        low(t - 2)
                    if not last and i >= 4:
                        dve.wait_ge(*lows_done(i - 4))
                    x = X[:, t, tokens(c)]
                    dve.scalar_tensor_tensor(out=x if last else norm_bufs[n][3][:, t % 4, :],
                                             in0=x, scalar=gains[:, t:t + 1], in1=rstd,
                                             op0=ALU.mult, op1=ALU.mult).then_inc(n_t, 1)
                if not last:
                    low(KT - 1)

            def add_tiles(n, ph, gains, base=X):
                nd = d_tiles(ph)

                def add(p, j, c):
                    m = bass.ds(p * 2 + j, 1)
                    dve.wait_ge(d_full, p * 6 + ((nd + j) * 3 + c + 1))
                    dve.tensor_tensor(X[:, m, tokens(c)].rearrange("p a n -> p (a n)"),
                                      base[:, m, tokens(c)].rearrange("p a n -> p (a n)"),
                                      ps[:, 3 + c, 0:CH], ALU.add).then_inc(d_read, 1)

                def tile(p, j):
                    for c in range(NCH):
                        add(p, j, c)
                    if n is not None:
                        for c in range(NCH):
                            add_square(n, p * 6 + (3 * j + c), c, c)

                with dve.Fori(0, KT // 2 - (n is not None)) as p:
                    tile(p, 0)
                    tile(p, 1)
                if n is None:
                    dve.wait_ge(d_read, 3 * (nd + KT))
                    return
                p = KT // 2 - 1
                tile(p, 0)
                for c in range(2):
                    add(p, 1, c)
                    add_square(n, p * 6 + 3 + c, c, c)
                dve.wait_ge(d_read, 3 * (nd + KT) - 1)
                scale(n, 0, gains)
                add(p, 1, 2)
                add_square(n, p * 6 + 5, 2, 2)
                dve.wait_ge(d_read, 3 * (nd + KT))
                scale(n, 1, gains)
                scale(n, 2, gains)

            clear_sums(0)
            dve.wait_ge(consts_in, 16 * 6)
            for c in range(NCH):
                for t in range(KT):
                    i = KT * c + t
                    add_square(0, i, c, i % 3)
                if c == 0:
                    scale(0, 0, g_cols["mix"])
            scale(0, 1, g_cols["mix"])
            scale(0, 2, g_cols["mix"])

            def transposed(dst, n, bank):
                w_ = P if n % 9 < 8 else NS
                dve.wait_ge(tr_full, n + 1)
                dve.tensor_copy(dst[0:w_, n % 9, :], ps[0:w_, bank, 0:W]).then_inc(tr_read, 1)

            dve.wait_ge(att_in, 16 * 6)
            link(dve.memset(qbd[:], 0.0))
            dve.wait_ge(a_read, 18)
            for hp in range(2):
                for h2 in range(2):
                    r = slice(64 * h2, 64 * h2 + 64)
                    ins = dve.tensor_copy(qbd[r, hp, :, h2, :], as_samples(q[r, hp, TP:T]))
            ins.then_inc(qbd_ready, 1)
            for n in range(9):
                transposed(vT, n, 6 + n % 2)
            dve.wait_ge(tr_read, 9)

            def biased(i):
                w, n = width(i), keys(i)
                dve.wait_ge(z_full, i + 1)
                if i >= 4:
                    dve.wait_ge(a_ready, i - 3)
                src, out = ps[0:n, z_bank(i), w], bufs(i)[0][0:n, w]
                if i < NU:
                    h = units[i][0]
                    dve.tensor_scalar(out, src, HD ** -0.5, sb_bias[:, h:h + 1], ALU.mult, ALU.add
                                      ).then_inc(z_read, 1)
                else:
                    dve.scalar_tensor_tensor(out=out, in0=src, scalar=HD ** -0.5, in1=bcol[0:n, :],
                                             op0=ALU.mult, op1=ALU.add).then_inc(z_read, 1)

            def exponent(i):
                w, n = width(i), keys(i)
                dve.wait_ge(later_full, i + 1)
                z = bufs(i)[0][0:n, w]
                bank = 3 + units[i][0] % 2 if i < NU else 3
                dve.wait_ge(z_read, i + 1)
                ins = dve.tensor_tensor(z, z, ps[0:n, bank, w], ALU.subtract)
                if on_diagonal(i):
                    link(ins)
                    m = bufs(i)[0][0:n, offset(i) if i < NU else 0:][:, 0:P]
                    ins = dve.tensor_tensor(m, m, (causal if i < NU else own)[0:n, 1, :], ALU.add)
                ins.then_inc(t_ready, 1)

            def softplus(i):
                w, n = width(i), keys(i)
                dve.wait_ge(l_ready, i + 1)
                if i >= 2:
                    dve.wait_ge(later_full, i)
                z, ln_part, out, _ = bufs(i)
                ins = dve.scalar_tensor_tensor(out=out[0:n, w], in0=z[0:n, w], scalar=0.0,
                                               in1=ln_part[0:n, w], op0=ALU.max, op1=ALU.add)
                if on_diagonal(i):
                    link(ins)
                    m = out[0:n, offset(i) if i < NU else 0:][:, 0:P]
                    ins = dve.tensor_tensor(m, m, (causal if i < NU else own)[0:n, 0, :], ALU.mult)
                ins.then_inc(sp_ready, 1)

            def output(i):
                dve.wait_ge(pv_done, i + 1)
                if i < NU:
                    h, qc, _ = units[i]
                    r = slice(HD * (h % 2), HD * (h % 2) + HD)
                    dve.tensor_copy(q[r, h // 2, qc * QC:(qc + 1) * QC], ps[r, 7, :]
                                    ).then_inc(o_read, 1)
                else:
                    for hp in range(2):
                        for h2 in range(2):
                            r = slice(64 * h2, 64 * h2 + 64)
                            src = ps[r, 7, hp * 64:(hp + 1) * 64].rearrange(
                                "p (b h t) -> p b h t", b=NB, h=2)[:, :, h2, :]
                            ins = dve.tensor_copy(as_samples(q[r, hp, TP:T]), src)
                    ins.then_inc(o_read, 1)

            biased(0)
            for i in range(NU + 3):
                if i >= 3 and is_last(i - 3):
                    output(i - 3)
                if i + 1 < NU:
                    biased(i + 1)
                if 1 <= i <= NU:
                    exponent(i - 1)
                if i < NU:
                    softplus(i)
            dve.wait_ge(o_read, chains_before(NU))

            def into_slot(s, src):
                link(dve.tensor_copy(slot_hi[:, s], src))
                dve.tensor_tensor(slot_lo[:, s], src, slot_hi[:, s], ALU.subtract
                                  ).then_inc(slot_ready, 1)

            def times_side(n, buf, pad, t):
                dve.wait_ge(a_read, 3 * (n + 1))
                dve.tensor_tensor(buf[:, pad:pad + TP], buf[:, pad:pad + TP], side[:, t, 0:TP],
                                  ALU.mult)
                dve.tensor_tensor(sample_cols(buf, pad), sample_cols(buf, pad),
                                  as_samples(side[:, t, TP:T]), ALU.mult).then_inc(prod_done, 1)

            def normed_block(blk):
                n = P if blk < 8 else NS
                x = vaT[0:n, blk, :]
                link(dve.reciprocal(stat[0:n, blk, 4:5], stat[0:n, blk, 4:5]))
                link(dve.tensor_scalar(x, x, stat[0:n, blk, 6:7], stat[0:n, blk, 4:5],
                                       ALU.subtract, ALU.mult))
                link(dve.tensor_tensor(x, x, lnv[0:n, 0, :], ALU.mult))
                dve.tensor_tensor(x, x, lnv[0:n, 1, :], ALU.add).then_inc(va_done, 1)

            def mixed(m):
                dve.wait_ge(mix_full, m + 1)
                if m < 4:
                    t, half = m // 2, m % 2
                    part = slice(half * 512, (half + 1) * 512)
                    dve.tensor_tensor(
                        va[:, t, part].rearrange("p (c n) -> p c n", c=4),
                        ps[:, 4 + 2 * half, :].rearrange("p (c n) -> p c n", c=4),
                        bsp[:, t, :].rearrange("p (c n) -> p c n", c=1).to_broadcast([P, 4, P]),
                        ALU.add).then_inc(mix_read, 1)
                    dve.wait_ge(mix_read, m + 1)
                    link(dve.tensor_tensor(u[:, t, part], u[:, t, part], va[:, t, part], ALU.mult))
                else:
                    dve.tensor_tensor(va[:, :, TP:T],
                                      ps[:, 4, 0:2 * NS].rearrange("p (t n) -> p t n", t=2),
                                      bss[:], ALU.add).then_inc(mix_read, 1)
                    dve.wait_ge(mix_read, m + 1)
                    link(dve.tensor_tensor(u[:, :, TP:T], u[:, :, TP:T], va[:, :, TP:T], ALU.mult))

            for s in range(SLOTS + 1):
                if s <= N_PAGES:
                    biased(NU + s)
                if 1 <= s <= N_PAGES + 1:
                    exponent(NU + s - 1)
                if s <= N_PAGES:
                    softplus(NU + s)
                if s == N_PAGES + 2:
                    output(STEPS - 1)
                    dve.wait_ge(o_read, chains_before(STEPS))
                    into_slot(0, q[:])
                    into_slot(1, u[:])
                if 2 <= s < 5:
                    for n in range(9 + 3 * (s - 2), 9 + 3 * (s - 1)):
                        blk = n - 9
                        rows = P if blk < 8 else NS
                        transposed(vaT, n, 4 + 2 * ((n - 3) % 2))
                        dve.wait_ge(tr_read, n + 1)
                        link(dve.bn_stats(stat[0:rows, blk, 0:6], vaT[0:rows, blk, :]))
                        dve.bn_aggr(stat[0:rows, blk, 6:8], stat[0:rows, blk, 0:6]
                                    ).then_inc(va_stat, 1)
                if s == 3:
                    dve.wait_ge(pv_done, NU + 1)
                    for t in range(2):
                        dve.memset(pb[:, t, 0:2], 0.0).then_inc(pads_ready, 1)
                        dve.memset(pcv[:, t, 0:CW - 1], 0.0).then_inc(pads_ready, 1)
                if s == 6:
                    dve.wait_ge(mixc_in, 16 * 5)
                    dve.wait_ge(va_std, 1)
                    for blk in range(9):
                        normed_block(blk)
                    dve.wait_ge(states_in, 16 * 4)
                    times_side(11, pb[:, 0, :], 2, 0)
                if s == 7:
                    for m in range(3):
                        mixed(m)
                if s == 8:
                    mixed(3)
                    mixed(4)
                    times_side(13, pb[:, 1, :], 2, 1)
                if s == 10:
                    times_side(15, pcv[:, 0, :], CW - 1, 0)
            times_side(17, pcv[:, 1, :], CW - 1, 1)

            def merge(p, j, a, dn, first, gate=gate):
                m = bass.ds(p * 2 + j, 1)
                for c in range(NCH):
                    dve.wait_ge(a_read, p * 6 + ((a + j) * 3 + c + 1))
                    dve.wait_ge(d_full, p * 6 + ((dn + j) * 3 + c + 1))
                    g = gate[:, c, :]
                    dve.tensor_tensor(g, g, ps[:, 3 + c, 0:CH], ALU.mult).then_inc(d_read, 1)
                    x = X[:, m, tokens(c)].rearrange("p a n -> p (a n)")
                    dve.wait_ge(d_read, p * 6 + ((dn + j) * 3 + c + 1))
                    if first:
                        dve.tensor_copy(x, g).then_inc(g_used, 1)
                    else:
                        dve.tensor_tensor(x, x, g, ALU.add).then_inc(g_used, 1)

            def taps(src, out_w, w, k0, k1):
                out = acc[:, 0:out_w]
                for i in range(k0, k1):
                    x = src[:, i:i + out_w]
                    if i == 0:
                        link(dve.tensor_scalar(out, x, w[:, 0:1], None, ALU.mult))
                    else:
                        link(dve.scalar_tensor_tensor(out=out, in0=x, scalar=w[:, i:i + 1], in1=out,
                                                      op0=ALU.mult, op1=ALU.add))

            def conv_b(t):
                def run():
                    n = LB - 2
                    if t == 0:
                        dve.wait_ge(a_read, 3 * 20)
                    taps(pb[:, t, :], n, conv_b_w[:, 3 * t:3 * t + 3], 0, 3)
                    link(dve.tensor_tensor(bg[:, t, 0:TP], bg[:, t, 0:TP], acc[:, 0:TP], ALU.mult))
                    link(dve.tensor_tensor(
                        as_samples(bg[:, t, TP:T]), as_samples(bg[:, t, TP:T]),
                        acc[:, TP:n].rearrange("p (b t) -> p b t", b=NB)[:, :, 2:], ALU.mult))
                return run

            def conv_c(t, k0, k1):
                def run():
                    n = LC - CW + 1
                    taps(pcv[:, t, :], n, conv_c_w[:, CW * t:CW * (t + 1)], k0, k1)
                    if k1 == CW:
                        if t == 0:
                            dve.wait_ge(out_state, 16 * 4)
                        link(dve.tensor_copy(cv[:, t, 0:TP], acc[:, 0:TP]))
                        ins = dve.tensor_copy(
                            as_samples(cv[:, t, TP:T]),
                            acc[:, TP:n].rearrange("p (b t) -> p b t", b=NB)[:, :, CW - 1:])
                        ins.then_inc(c_conv, 1)
                        dve.wait_ge(c_conv, t + 1)
                return run

            def several(fs):
                def run():
                    for f in fs:
                        f()
                return run

            cuts = [0, 5, 10, 15, 20, 25, CW]
            steps = [conv_b(0), conv_b(1)] + [conv_c(0, a, b) for a, b in zip(cuts, cuts[1:])]
            steps += [lambda: into_slot(0, bg[:])]
            steps += [conv_c(1, a, b) for a, b in zip(cuts, cuts[1:])] + [lambda: None]
            for br in range(4):
                a, dn = N_MIX + 8 * br, 8 * br
                if br < 2:
                    for m in range(KT):
                        merge(m // 2, m % 2, a, dn, br == 0)
                        steps[8 * br + m]()
                elif br == 2:
                    for m in range(KT):
                        merge(m // 2, m % 2, a, dn, False)
                        c = m // 2
                        if c < NCH and m % 2 == 0:
                            dve.wait_ge(c_mean, c + 1)
                            for t in range(2):
                                ins = dve.tensor_tensor(cv[:, t, tokens(c)], cv[:, t, tokens(c)],
                                                        ps[:, 6, 0:CH], ALU.subtract)
                            ins.then_inc(c_cent, 1)
                            dve.wait_ge(c_cent, c + 1)
                        elif c < NCH:
                            dve.wait_ge(c_std, c + 1)
                            link(dve.reciprocal(cstd[:], cstd[:]))
                            for t in range(2):
                                ins = dve.tensor_tensor(cv[:, t, tokens(c)], cv[:, t, tokens(c)],
                                                        cstd[:], ALU.mult)
                            ins.then_inc(c_norm, 1)
                            dve.wait_ge(c_norm, c + 1)
                        elif m == 2 * NCH:
                            dve.wait_ge(c_act, 2)
                            into_slot(1, cv[:])
                else:
                    with dve.Fori(0, KT // 2) as p:
                        for j in range(2):
                            merge(p, j, a, dn, False, gate_late)
            for c in range(NCH):
                dve.wait_ge(m_high, c + 1)
                dve.tensor_tensor(h_lo[:, :, tokens(c)], X[:, :, tokens(c)], h_hi[:, :, tokens(c)],
                                  ALU.subtract).then_inc(m_ready, 1)
            dve.wait_ge(m_ready, NCH)

            clear_sums(1)
            dve.wait_ge(x2_in, 16 * KT)
            add_tiles(1, 2, g_cols["ffn"], x_again)
            for t in (6, 7):
                dve.wait_ge(*lows_done(KT * (2 * NCH - 1) + t))
            dve.memset(up[:, 0, 0:2], 0.0).then_inc(up_used, 1)
            dve.memset(up[:, 1, 0:2], 0.0).then_inc(up_used, 1)

            def convolve(f, j, a, tile):
                one = bass.ds(f * 2 + (tile + j), 1)
                dve.wait_ge(a_read, f * 6 + (a + j) * 3 + 3)
                n = LB - 2
                out, x = cu[:, j, :], up[:, j, :]
                w = ffn_w[:, one, :].rearrange("p a n -> p (a n)")
                dve.tensor_copy(ffn_last[:, one, :].rearrange("p a (b t) -> p (a b) t", t=2),
                                last_cols(x, 2))
                link(dve.tensor_scalar(out, x[:, 0:n], w[:, 0:1], None, ALU.mult))
                link(dve.scalar_tensor_tensor(out=out, in0=x[:, 1:1 + n], scalar=w[:, 1:2], in1=out,
                                              op0=ALU.mult, op1=ALU.add))
                dve.scalar_tensor_tensor(out=out, in0=x[:, 2:2 + n], scalar=w[:, 2:3], in1=out,
                                         op0=ALU.mult, op1=ALU.add).then_inc(up_used, 1)

            def hidden(f, g, tile, slot):
                convolve(f, 0, normed_tiles(UP[g]), 2 * tile)
                convolve(f, 1, normed_tiles(UP[g]), 2 * tile)
                dve.wait_ge(up_used, f * 2 + (2 * tile + 4))
                dve.wait_ge(ga_act, f + (tile + 1))
                dve.tensor_tensor(cu[:, 1, :], cu[:, 1, :], cu[:, 0, :], ALU.mult
                                  ).then_inc(prod_ready, 1)
                dve.wait_ge(hid_h, f + (tile + 1))
                one = bass.ds(slot, 1)
                dve.tensor_tensor(hid_lo[:, one, 0:TP].rearrange("p a n -> p (a n)"),
                                  cu[:, 1, 0:TP],
                                  hid_hi[:, one, 0:TP].rearrange("p a n -> p (a n)"),
                                  ALU.subtract)
                dve.tensor_tensor(
                    as_samples(hid_lo[:, one, TP:T].rearrange("p a n -> p (a n)")),
                    cu[:, 1, TP:].rearrange("p (b t) -> p b t", b=NB)[:, :, 2:],
                    as_samples(hid_hi[:, one, TP:T].rearrange("p a n -> p (a n)")),
                    ALU.subtract).then_inc(hid_ready, 1)

            f0 = 0
            for g in range(len(GROUPS)):
                last = g == len(GROUPS) - 1
                own_tiles = sum(GROUPS[:g + 1]) - f0
                with Loop(0, own_tiles, 4) as f:
                    hidden(f, g, f0, f)
                if not last:
                    hidden(own_tiles, g, f0, AHEAD[g + 1])
                f0 += UPS[g]
                if last:
                    dve.wait_ge(hid_ready, FT)
                    clear_sums(2)
                    dve.wait_ge(p_high, 2)
                    for t in range(2):
                        dve.tensor_tensor(p_lo[t][:], p_in[t][:], p_hi[t][:], ALU.subtract
                                          ).then_inc(p_ready, 1)
                add_tiles(2 if last else None, DOWN[g], g_cols["ple"])

            clear_sums(3)
            with dve.Fori(0, KT // 2) as p:
                for j in range(2):
                    merge(p, j, normed_tiles(PLE), d_tiles(PLE), False, gate_late)
                    for c in range(NCH):
                        add_square(3, p * 6 + (3 * j + c), c, c)
            dve.wait_ge(g_used, 3 * (N_GATE + KT))
            for c in range(NCH):
                scale(3, c, g_cols["final"], last=True)


def tiles(w, n0, n1):
    kt = w.shape[0] // P
    return w[:, n0:n1].reshape(kt, P, (n1 - n0) // P, P).transpose(2, 1, 0, 3)


def feature_major(a, n):
    return a.reshape(-1, n, P).transpose(2, 1, 0)


def layout(i):
    f = np.float32
    w_in, w_br, w_up, w_down = i["w_in"][0], i["w_br"][0], i["w_up"][0], i["w_down"][0]
    a0, b0, c0, d0, g0 = 0, 512, 1280, 1792, 2560
    mix = [(d0, 6), (a0 + 256, 2), (a0, 2)]
    mix += [(b0 + 256, 1), (b0 + 512, 1), (b0 + 384, 1), (b0 + 640, 1)]
    mix += [(c0, 1), (c0 + 256, 1), (c0 + 128, 1), (c0 + 384, 1), (b0, 2)]
    w_mix = np.concatenate([tiles(w_in, o, o + n * P) for o, n in mix])
    gates = []
    for br in (3, 0, 1, 2):
        o = g0 + br * D_MODEL
        gates.append(np.concatenate([tiles(w_in, o, o + D_MODEL), tiles(w_br[br], 0, D_MODEL)], axis=2))
    w_upt = np.stack([tiles(w_up, 0, D_FF), tiles(w_up, D_FF, 2 * D_FF)], axis=1)
    downs = np.zeros((len(GROUPS) * KT, P, max(GROUPS), P), f)
    f0 = 0
    for n, g in enumerate(GROUPS):
        downs[n * KT:(n + 1) * KT, :, :g] = tiles(w_down[f0 * P:(f0 + g) * P], 0, D_MODEL)
        f0 += g
    w_ple = np.concatenate([tiles(i["w_ple_gate"][0], 0, D_MODEL), tiles(i["w_ple"][0], 0, D_MODEL)],
                           axis=2)
    flat = lambda a: np.ascontiguousarray(a).reshape(a.shape[0], P, -1)
    x = np.concatenate([i["x_prompt"].reshape(TP, D_MODEL), i["x_sample"].reshape(NS, D_MODEL)])
    p = np.concatenate([i["p_prompt"].reshape(TP, W), i["p_sample"].reshape(NS, W)])
    x = feature_major(x, KT).reshape(P, KT, NCH, CH).transpose(2, 0, 1, 3)
    small = np.zeros((P, 256), f)
    for n, g in enumerate(("g_mix", "g_ffn", "g_ple", "g_final")):
        small[:, 8 * n:8 * n + 8] = i[g].reshape(KT, P).T
    small[:, 32] = EPS
    small[:, 33:37] = i["sb_bias"][0]
    small[:, 37:39] = i["ln_c_g"][0].reshape(2, P).T
    small[:, 39:41] = i["ln_c_b"][0].reshape(2, P).T
    small[:, 41:47] = i["conv_b_w"][0].reshape(3, 2, P).transpose(2, 1, 0).reshape(P, 6)
    small[:, 47:47 + 2 * CW] = i["conv_c_w"][0].reshape(CW, 2, P).transpose(2, 1, 0).reshape(P, -1)
    small[:, 110] = 1.0
    ffn_w = i["ffn_conv_w"][0].reshape(3, 2, FT, P).transpose(3, 2, 1, 0).reshape(P, 2 * FT, 3)
    ffn_state = i["state_ffn_conv"][0].reshape(NB, 2, 2, FT, P).transpose(4, 3, 2, 0, 1)
    k_, q_ = np.arange(P)[:, None], np.arange(P)[None, :]
    later = (q_ > k_).astype(f)
    causal = np.stack([later, np.where(q_ > k_, 0, NEG).astype(f)], axis=1)
    col = np.arange(P)
    cb, ct = (col // 8) % NB, col % TS
    kb, kt_ = np.arange(NS)[:, None] // TS, np.arange(NS)[:, None] % TS
    ok = (kb == cb[None]) & (kt_ < ct[None])
    own = np.zeros((P, 2, P), f)
    own[:NS, 0] = ok
    own[:NS, 1] = np.where(ok, 0, NEG)
    bias = i["sb_bias"][0].reshape(2, 1, 2, 1)
    bcol = np.broadcast_to(np.broadcast_to(bias, (2, NB, 2, TS)).reshape(1, P), (P, P))
    lnv = np.stack([np.broadcast_to(i[n][0], (P, W)) for n in ("ln_v_g", "ln_v_b")], axis=1)
    w_sp, b_sp = i["w_sp"][0], i["b_sp"][0]
    bsp = np.broadcast_to(b_sp.reshape(2, 2, 1, P), (2, 2, 64, P)).reshape(2, P, P).transpose(1, 0, 2)
    bss = np.broadcast_to(bsp[:, :, None, :TS], (P, 2, NB, TS)).reshape(P, 2, NS)
    wss = np.zeros((NB, TS, 4, NB, TS), f)
    for b in range(NB):
        wss[b, :, :, b, :] = w_sp[:, :TS, :TS].transpose(2, 0, 1)
    out = dict(
        x=x, p=feature_major(p, 2), small=small, ident=np.eye(P, dtype=f),
        mean1024=np.full((P, P), 1 / D_MODEL, f), mean256=np.full((P, P), 1 / W, f),
        ffn_w=ffn_w, ffn_state=ffn_state.reshape(P, 2 * FT, 2 * NB),
        tri=(k_ >= q_).astype(f), comp=(k_ < q_).astype(f), causal=causal, own=own, bcol=bcol,
        ptab=i["page_table"].reshape(1, -1).astype(np.int32),
        cache_kT=i["cache_k"][0].reshape(N_PHYS, P, 2, P).transpose(0, 3, 2, 1).reshape(N_PHYS, P, W),
        cache_v=i["cache_v"][0].reshape(N_PHYS, P, W),
        state_b=i["state_conv_b"][0].reshape(NB, 2, 2, P).transpose(2, 3, 0, 1),
        state_c=i["state_conv_c"][0].reshape(NB, CW - 1, 2, P).transpose(2, 3, 0, 1),
        lnv=lnv, wsp=w_sp.transpose(2, 0, 1), bsp=bsp, bss=bss, wss=wss.reshape(NS, 4, NS),
        w_mix=flat(w_mix), w_gate=flat(np.concatenate(gates)), w_o=flat(tiles(i["w_o"][0], 0, D_MODEL)),
        w_up=flat(w_upt.reshape(2 * FT, P, KT, P)), w_down=flat(downs), w_ple=flat(w_ple))
    return {n: np.ascontiguousarray(a) for n, a in out.items()}


OUTS = dict(y=(KT, P, T), k_out=(P, 2, T), v_out=(P, 2, T), va_out=(NS, W), b_last=(2, P, NB + 1, 2),
            c_last=(2, P, NB + 1, CW - 1), ffn_last=(P, 2 * FT, 2 * (NB + 1)))


def kernel(**inputs):
    import concourse.bacc as bacc
    from concourse.bass_utils import run_bass_kernel_spmd

    nc = bacc.Bacc("TRN2", target_bir_lowering=False, num_devices=1)
    arrays = layout({n: np.asarray(a) for n, a in inputs.items()})
    d = {n: nc.dram_tensor(n + "_dram", a.shape, mybir.dt.from_np(a.dtype), kind="ExternalInput").ap()
         for n, a in arrays.items()}
    for n, shape in OUTS.items():
        d[n] = nc.dram_tensor(n + "_dram", shape, F32, kind="ExternalOutput").ap()
    hybrid_layer(nc, d)
    r = run_bass_kernel_spmd(nc, [{n + "_dram": a for n, a in arrays.items()}], core_ids=[0]).results[0]
    r = {n: np.asarray(r[n + "_dram"]) for n in OUTS}
    y = r["y"].reshape(D_MODEL, T).T
    kv = [r[n].transpose(2, 1, 0).reshape(T, HEADS, HD) for n in ("k_out", "v_out")]
    new = [a[:TP].reshape(1, 1, TP, HEADS, HD) for a in kv]
    new += [a[TP:].reshape(1, NB, TS, HEADS, HD) for a in kv]
    last_b = r["b_last"].transpose(2, 3, 0, 1).reshape(NB + 1, 2, W)
    last_c = r["c_last"].transpose(2, 3, 0, 1).reshape(NB + 1, CW - 1, W)
    last_f = r["ffn_last"].reshape(P, FT, 2, NB + 1, 2).transpose(3, 4, 2, 1, 0).reshape(NB + 1, 2, -1)
    states = [last_b, last_c, last_f]
    out = [y[:TP].reshape(1, TP, D_MODEL), y[TP:].reshape(NB, TS, D_MODEL), new[0], new[1]]
    out += [s[None, :1] for s in states]
    out += [new[2], new[3], r["va_out"].reshape(1, NB, TS, W)]
    out += [s[None, 1:] for s in states]
    return tuple(np.ascontiguousarray(a) for a in out)
```
